# Optimizing a Trainium2 kernel written in Bass

```python
import math
import jax, jax.numpy as jnp
from jax import lax
import numpy as np

D_MODEL = 1024
BATCH = 1
SEQ = 256
DEPTH = 2

D_CONV = D_MODEL
CONV_GROUPS = 8
SHORT_CONV_K = 3
D_RNN = D_MODEL
RNN_HEADS = 4
RNN_HEAD_DIM = D_RNN // RNN_HEADS
RNN_CONV_K = 4
LRU_C = 8.0
N_BRANCH = 2
D_FF = 2816
D_IN = 3 * D_CONV + 2 * D_RNN + N_BRANCH * D_MODEL
SPLITS = (D_CONV, 2 * D_CONV, 3 * D_CONV, 3 * D_CONV + D_RNN, 3 * D_CONV + 2 * D_RNN)
ALPHA = (2.0 * DEPTH) ** 0.25
BETA = (8.0 * DEPTH) ** -0.25
LN_EPS = 1e-5


def layer_norm(x, g, b):
    xf = x.astype(jnp.float32)
    mu = jnp.mean(xf, axis=-1, keepdims=True)
    var = jnp.mean(jnp.square(xf - mu), axis=-1, keepdims=True)
    y = (xf - mu) * lax.rsqrt(var + LN_EPS)
    return (y * g.astype(jnp.float32) + b.astype(jnp.float32)).astype(x.dtype)

def causal_depthwise_conv(x, w, k):
    s = x.shape[1]
    xp = jnp.pad(x, ((0, 0), (k - 1, 0), (0, 0)))
    out = xp[:, 0:s, :] * w[0]
    for i in range(1, k):
        out = out + xp[:, i:i + s, :] * w[i]
    return out

def swiglu(x, w1, w2):
    g, u = jnp.split(x @ w1, 2, axis=-1)
    return (jax.nn.silu(g) * u) @ w2

def rg_lru(x, gate_in, gate_rec, a_param):
    s = x.shape[1]
    log_a = -LRU_C * gate_rec * jax.nn.softplus(-a_param)
    a = jnp.exp(log_a)
    mult = jnp.sqrt(-jnp.expm1(2.0 * log_a))
    is_start = (jnp.arange(s) == 0)[None, :, None]
    mult = jnp.where(is_start, 1.0, mult)
    b = x * gate_in * mult

    def combine(left, right):
        a1, b1 = left
        a2, b2 = right
        return a1 * a2, a2 * b1 + b2

    _, h = lax.associative_scan(combine, (a, b), axis=1)
    return h

def hybrid_mixer(x, w_in, b_merge, sc_w, rc_w, rc_b, rg_w, rg_b, a_param,
                 w_out_conv, w_out_rnn, w_o):
    bsz, s, _ = x.shape
    proj = x @ w_in
    b_gate, c_gate, v, x_r, y_r, g_logits = jnp.split(proj, SPLITS, axis=-1)

    y_a = (b_gate * causal_depthwise_conv(c_gate * v, sc_w, SHORT_CONV_K)) @ w_out_conv

    xc = causal_depthwise_conv(x_r, rc_w, RNN_CONV_K) + rc_b
    xh = xc.reshape(bsz, s, RNN_HEADS, RNN_HEAD_DIM)
    gates = jnp.einsum('bshi,ghij->gbshj', xh, rg_w).reshape(2, bsz, s, D_RNN)
    gates = jax.nn.sigmoid((gates + rg_b[:, None, None, :]).astype(jnp.float32))
    h = rg_lru(xc.astype(jnp.float32), gates[0], gates[1],
               a_param.astype(jnp.float32)).astype(x.dtype)
    y_b = (h * jax.nn.gelu(y_r)) @ w_out_rnn

    g_a, g_b = jnp.split(jax.nn.sigmoid(g_logits + b_merge), 2, axis=-1)
    return (g_a * y_a + g_b * y_b) @ w_o

def first_inputs(seed: int = 0) -> dict:
    key = jax.random.key(seed)
    ks = jax.random.split(key, 20)
    f32 = jnp.float32
    nrm = lambda k, shape, scale: jax.random.normal(k, shape, f32) * scale

    x = jax.random.normal(ks[0], (BATCH, SEQ, D_MODEL), f32)
    w_in = nrm(ks[1], (DEPTH, D_MODEL, D_IN), D_MODEL ** -0.5)
    b_merge = nrm(ks[2], (DEPTH, N_BRANCH * D_MODEL), 0.1)
    sc_w = nrm(ks[3], (DEPTH, SHORT_CONV_K, D_CONV), SHORT_CONV_K ** -0.5)
    rc_w = nrm(ks[4], (DEPTH, RNN_CONV_K, D_RNN), RNN_CONV_K ** -0.5)
    rc_b = nrm(ks[5], (DEPTH, D_RNN), 0.02)
    rg_w = nrm(ks[6], (DEPTH, 2, RNN_HEADS, RNN_HEAD_DIM, RNN_HEAD_DIM), RNN_HEAD_DIM ** -0.5)
    rg_b = nrm(ks[7], (DEPTH, 2, D_RNN), 0.1)
    u = jax.random.uniform(ks[8], (DEPTH, D_RNN), f32, 0.9, 0.999)
    s_a = u ** (1.0 / LRU_C)
    a_param = jnp.log(s_a) - jnp.log1p(-s_a)
    w_out_conv = nrm(ks[9], (DEPTH, D_CONV, D_MODEL), D_CONV ** -0.5)
    w_out_rnn = nrm(ks[10], (DEPTH, D_RNN, D_MODEL), D_RNN ** -0.5)
    w_o = nrm(ks[11], (DEPTH, D_MODEL, D_MODEL), BETA * D_MODEL ** -0.5)
    ffn_w1 = nrm(ks[12], (DEPTH, 2, D_MODEL, 2 * D_FF), D_MODEL ** -0.5)
    ffn_w2 = nrm(ks[13], (DEPTH, 2, D_FF, D_MODEL), BETA * D_FF ** -0.5)
    ln_g = 1.0 + nrm(ks[14], (DEPTH, 3, D_MODEL), 0.02)
    ln_b = nrm(ks[15], (DEPTH, 3, D_MODEL), 0.02)
    return {"x": x, "w_in": w_in, "b_merge": b_merge, "sc_w": sc_w, "rc_w": rc_w,
            "rc_b": rc_b, "rg_w": rg_w, "rg_b": rg_b, "a_param": a_param,
            "w_out_conv": w_out_conv, "w_out_rnn": w_out_rnn, "w_o": w_o,
            "ffn_w1": ffn_w1, "ffn_w2": ffn_w2, "ln_g": ln_g, "ln_b": ln_b}

def first_block(x, w_in, b_merge, sc_w, rc_w, rc_b, rg_w, rg_b, a_param,
              w_out_conv, w_out_rnn, w_o, ffn_w1, ffn_w2, ln_g, ln_b):
    for l in range(DEPTH):
        x = layer_norm(ALPHA * x + 0.5 * swiglu(x, ffn_w1[l, 0], ffn_w2[l, 0]),
                       ln_g[l, 0], ln_b[l, 0])
        mix = hybrid_mixer(x, w_in[l], b_merge[l], sc_w[l], rc_w[l], rc_b[l], rg_w[l],
                           rg_b[l], a_param[l], w_out_conv[l], w_out_rnn[l], w_o[l])
        x = layer_norm(ALPHA * x + mix, ln_g[l, 1], ln_b[l, 1])
        x = layer_norm(ALPHA * x + 0.5 * swiglu(x, ffn_w1[l, 1], ffn_w2[l, 1]),
                       ln_g[l, 2], ln_b[l, 2])
    return x


DEPTH_2 = 1

CHUNK = 64
QBLK = 128
EPS = 1e-6

REC_HEADS = 4
REC_DK = 128
REC_DV = 128
REC_W = REC_HEADS * REC_DV
ATT_HEADS = 8
ATT_DH = 64
ATT_W = ATT_HEADS * ATT_DH
IDX_HEADS = 8
IDX_DIM = 64
TOPK_MAX = 256
NUM_BUCKETS = 32
MAX_DISTANCE = 128
N_GROUPS = 4
EXPERTS_PER_GROUP = 4
N_EXPERTS = N_GROUPS * EXPERTS_PER_GROUP
TOP_K_EXPERTS = 2
D_EXPERT = 512

MIX_W = REC_W + ATT_W
IN_SIZES = (REC_HEADS * REC_DK,
            REC_HEADS * REC_DK,
            REC_W,
            REC_W,
            ATT_W, ATT_W, ATT_W,
            IDX_HEADS * IDX_DIM,
            IDX_DIM,
            IDX_HEADS)
D_IN_2 = int(sum(IN_SIZES))
IN_OFFSETS = tuple(int(o) for o in np.cumsum(IN_SIZES)[:-1])


def _rms(x, g):
    xf = x.astype(jnp.float32)
    y = xf * lax.rsqrt(jnp.mean(xf * xf, axis=-1, keepdims=True) + EPS)
    return (y * g.astype(jnp.float32)).astype(x.dtype)

def _layernorm(x, g, b):
    xf = x.astype(jnp.float32)
    mu = jnp.mean(xf, axis=-1, keepdims=True)
    var = jnp.mean(jnp.square(xf - mu), axis=-1, keepdims=True)
    y = (xf - mu) * lax.rsqrt(var + EPS)
    return (y * g.astype(jnp.float32) + b.astype(jnp.float32)).astype(x.dtype)

def _t5_bucket(rel):
    nb = NUM_BUCKETS // 2
    max_exact = nb // 2
    ret = jnp.where(rel > 0, nb, 0)
    n = jnp.abs(rel)
    nf = jnp.maximum(n, 1).astype(jnp.float32)
    large = max_exact + (jnp.log(nf / max_exact) / np.log(MAX_DISTANCE / max_exact)
                         * (nb - max_exact)).astype(jnp.int32)
    large = jnp.minimum(large, nb - 1)
    return ret + jnp.where(n < max_exact, n, large)

def _hgrn2(q_raw, f_raw, i_raw, g_raw, lb, out_g):
    B, S, _ = q_raw.shape
    nc = S // CHUNK
    f32 = jnp.float32
    q = jax.nn.silu(q_raw.astype(f32))
    f = lb + (1.0 - lb) * jax.nn.sigmoid(f_raw.astype(f32))
    k = 1.0 - f
    lf = jnp.log(f)
    v = i_raw.astype(f32)

    def to_chunks(a, d):
        return a.reshape(B, nc, CHUNK, REC_HEADS, d).transpose(1, 0, 3, 2, 4)

    tril = jnp.tril(jnp.ones((CHUNK, CHUNK), bool))[:, :, None]

    def step(state, inp):
        qc, kc, vc, lfc = inp
        b = jnp.cumsum(lfc, axis=2)
        diff = b[:, :, :, None, :] - b[:, :, None, :, :]
        decay = jnp.where(tril, jnp.exp(jnp.where(tril, diff, 0.0)), 0.0)
        attn = jnp.einsum('bhtk,bhsk,bhtsk->bhts', qc, kc, decay)
        o = (jnp.einsum('bhts,bhsv->bhtv', attn, vc)
             + jnp.einsum('bhtk,bhkv->bhtv', qc * jnp.exp(b), state))
        b_end = b[:, :, -1:, :]
        state = (jnp.exp(b_end[:, :, 0, :])[..., None] * state
                 + jnp.einsum('bhsk,bhsv->bhkv', kc * jnp.exp(b_end - b), vc))
        return state, o

    s0 = jnp.zeros((B, REC_HEADS, REC_DK, REC_DV), f32)
    _, o = lax.scan(step, s0, (to_chunks(q, REC_DK), to_chunks(k, REC_DK),
                               to_chunks(v, REC_DV), to_chunks(lf, REC_DK)))
    o = o.transpose(1, 0, 3, 2, 4).reshape(B, S, REC_HEADS, REC_DV)
    o = _rms(o, out_g.reshape(REC_HEADS, REC_DV))
    gate = jax.nn.silu(g_raw.astype(f32)).reshape(B, S, REC_HEADS, REC_DV)
    return (o * gate).reshape(B, S, REC_W).astype(q_raw.dtype)

def _dsa_attention(q, k, v, iq, ik, iw, rel_bias):
    B, S = q.shape[0], q.shape[1]
    nb = S // QBLK
    k_sel = min(TOPK_MAX, S // 4)
    key_chunk = jnp.arange(S) // CHUNK
    ikf = ik.astype(jnp.float32)

    def blocks(a):
        return a.reshape((B, nb, QBLK) + a.shape[2:]).swapaxes(0, 1)

    def one_block(args):
        bi, qb, iqb, iwb = args
        t = bi * QBLK + jnp.arange(QBLK)
        t_chunk = t // CHUNK
        sc = jnp.einsum('bqhd,bsd->bqhs', iqb.astype(jnp.float32), ikf) * IDX_DIM ** -0.5
        score = jnp.einsum('bqhs,bqh->bqs', jax.nn.relu(sc), iwb.astype(jnp.float32))
        adm = key_chunk[None, :] <= t_chunk[:, None]
        score = jnp.where(adm[None], score, -jnp.inf)
        _, idx = lax.top_k(score, k_sel)
        valid = (idx // CHUNK) <= t_chunk[None, :, None]
        kg = jax.vmap(lambda a, j: a[j])(k, idx)
        vg = jax.vmap(lambda a, j: a[j])(v, idx)
        logits = jnp.einsum('bqhd,bqkhd->bqhk', qb, kg).astype(jnp.float32) * ATT_DH ** -0.5
        bias = rel_bias[_t5_bucket(idx - t[None, :, None])]
        logits = logits + jnp.swapaxes(bias, 2, 3).astype(jnp.float32)
        logits = jnp.where(valid[:, :, None, :], logits, -jnp.inf)
        p = jax.nn.softmax(logits, axis=-1).astype(vg.dtype)
        return jnp.einsum('bqhk,bqkhd->bqhd', p, vg)

    out = lax.map(one_block, (jnp.arange(nb), blocks(q), blocks(iq), blocks(iw)))
    return out.swapaxes(0, 1).reshape(B, S, ATT_HEADS, ATT_DH)

def _hier_moe(h, w_rg, b_rg, w_re, b_re, w1, w3, w2):
    B, S, D = h.shape
    hf = h.reshape(B * S, D)
    g_logits = (hf @ w_rg + b_rg).astype(jnp.float32)
    p_group = jax.nn.softmax(g_logits, axis=-1)
    g_top = jnp.argmax(g_logits, axis=-1)
    gate_g = jnp.take_along_axis(p_group, g_top[:, None], axis=-1)
    e_logits = (hf @ w_re + b_re).astype(jnp.float32).reshape(-1, N_GROUPS, EXPERTS_PER_GROUP)
    e_in = jnp.take_along_axis(e_logits, g_top[:, None, None], axis=1)[:, 0]
    top_v, top_j = lax.top_k(e_in, TOP_K_EXPERTS)
    w_sel = jax.nn.softmax(top_v, axis=-1) * gate_g
    e_id = g_top[:, None] * EXPERTS_PER_GROUP + top_j
    combine = jnp.einsum('nk,nke->ne', w_sel,
                         jax.nn.one_hot(e_id, N_EXPERTS, dtype=jnp.float32)).astype(h.dtype)
    y = jnp.zeros_like(hf)
    for e in range(N_EXPERTS):
        he = jax.nn.silu(hf @ w1[e]) * (hf @ w3[e])
        y = y + combine[:, e:e + 1] * (he @ w2[e])
    return y.reshape(B, S, D)

def second_inputs(seed: int = 0) -> dict:
    key = jax.random.key(seed)
    ks = jax.random.split(key, 24)
    f32 = jnp.float32

    def nrm(k, shape, s):
        return jax.random.normal(k, shape, f32) * s

    D = D_MODEL
    return {
        'x': nrm(ks[0], (BATCH, SEQ, D), 1.0),
        'c': nrm(ks[1], (BATCH, D), 1.0),
        'w_ada': nrm(ks[2], (DEPTH_2, D, 6 * D), 0.5 * D ** -0.5),
        'b_ada': nrm(ks[3], (DEPTH_2, 6 * D), 0.02),
        'norm1_g': 1.0 + nrm(ks[4], (DEPTH_2, D), 0.02),
        'norm2_g': 1.0 + nrm(ks[5], (DEPTH_2, D), 0.02),
        'w_in': nrm(ks[6], (DEPTH_2, D, D_IN_2), D ** -0.5),
        'lb_logits': nrm(ks[7], (DEPTH_2 + 1, REC_HEADS * REC_DK), 0.5),
        'rec_out_g': 1.0 + nrm(ks[8], (DEPTH_2, REC_W), 0.02),
        'q_norm_g': 1.0 + nrm(ks[9], (DEPTH_2, ATT_DH), 0.02),
        'k_norm_g': 1.0 + nrm(ks[10], (DEPTH_2, ATT_DH), 0.02),
        'idx_k_norm_g': 1.0 + nrm(ks[11], (DEPTH_2, IDX_DIM), 0.02),
        'idx_k_norm_b': nrm(ks[12], (DEPTH_2, IDX_DIM), 0.02),
        'attn_out_g': 1.0 + nrm(ks[13], (DEPTH_2, ATT_W), 0.02),
        'rel_bias': nrm(ks[14], (NUM_BUCKETS, ATT_HEADS), 0.5),
        'w_out': nrm(ks[15], (DEPTH_2, MIX_W, D), MIX_W ** -0.5),
        'w_rg': nrm(ks[16], (DEPTH_2, D, N_GROUPS), D ** -0.5),
        'b_rg': nrm(ks[17], (DEPTH_2, N_GROUPS), 0.01),
        'w_re': nrm(ks[18], (DEPTH_2, D, N_EXPERTS), D ** -0.5),
        'b_re': nrm(ks[19], (DEPTH_2, N_EXPERTS), 0.01),
        'w1': nrm(ks[20], (DEPTH_2, N_EXPERTS, D, D_EXPERT), D ** -0.5),
        'w3': nrm(ks[21], (DEPTH_2, N_EXPERTS, D, D_EXPERT), D ** -0.5),
        'w2': nrm(ks[22], (DEPTH_2, N_EXPERTS, D_EXPERT, D), D_EXPERT ** -0.5),
    }

def second_block(x, c, w_ada, b_ada, norm1_g, norm2_g, w_in, lb_logits, rec_out_g,
              q_norm_g, k_norm_g, idx_k_norm_g, idx_k_norm_b, attn_out_g, rel_bias,
              w_out, w_rg, b_rg, w_re, b_re, w1, w3, w2):
    B, S, D = x.shape
    lb_all = jnp.cumsum(jax.nn.softmax(lb_logits.astype(jnp.float32), axis=0), axis=0)
    for l in range(DEPTH_2):
        mod = jax.nn.silu(c) @ w_ada[l] + b_ada[l]
        sh1, sc1, g1, sh2, sc2, g2 = jnp.split(mod, 6, axis=-1)

        h = _rms(x, norm1_g[l]) * (1.0 + sc1[:, None, :]) + sh1[:, None, :]
        z = h @ w_in[l]
        rq, rf, ri, rg, aq, ak, av, iq, ik, iw = jnp.split(z, IN_OFFSETS, axis=-1)

        rec = _hgrn2(rq, rf, ri, rg, lb_all[l], rec_out_g[l])

        aq = _rms(aq.reshape(B, S, ATT_HEADS, ATT_DH), q_norm_g[l])
        ak = _rms(ak.reshape(B, S, ATT_HEADS, ATT_DH), k_norm_g[l])
        av = av.reshape(B, S, ATT_HEADS, ATT_DH)
        iq = iq.reshape(B, S, IDX_HEADS, IDX_DIM)
        ik = _layernorm(ik, idx_k_norm_g[l], idx_k_norm_b[l])
        iw = iw * IDX_HEADS ** -0.5
        att = _dsa_attention(aq, ak, av, iq, ik, iw, rel_bias)
        att = _rms(att, attn_out_g[l].reshape(ATT_HEADS, ATT_DH)).reshape(B, S, ATT_W)

        mix = jnp.concatenate([rec, att.astype(rec.dtype)], axis=-1) @ w_out[l]
        x = x + g1[:, None, :] * mix

        h2 = _rms(x, norm2_g[l]) * (1.0 + sc2[:, None, :]) + sh2[:, None, :]
        x = x + g2[:, None, :] * _hier_moe(h2, w_rg[l], b_rg[l], w_re[l], b_re[l],
                                           w1[l], w3[l], w2[l])
    return x


def setup_inputs(seed=0):
    out = dict(first_inputs(seed))
    for name, value in second_inputs(seed + 1).items():
        if name != "x":
            out[name + "_2"] = value
    return out


def reference(
    x, w_in, b_merge, sc_w, rc_w, rc_b, rg_w, rg_b, a_param, w_out_conv, w_out_rnn, w_o, ffn_w1,
    ffn_w2, ln_g, ln_b, c_2, w_ada_2, b_ada_2, norm1_g_2, norm2_g_2, w_in_2, lb_logits_2,
    rec_out_g_2, q_norm_g_2, k_norm_g_2, idx_k_norm_g_2, idx_k_norm_b_2, attn_out_g_2,
    rel_bias_2, w_out_2, w_rg_2, b_rg_2, w_re_2, b_re_2, w1_2, w3_2, w2_2,
):
    x = first_block(
        x, w_in, b_merge, sc_w, rc_w, rc_b, rg_w, rg_b, a_param, w_out_conv, w_out_rnn, w_o,
        ffn_w1, ffn_w2, ln_g, ln_b,
    )
    return second_block(
        x, c_2, w_ada_2, b_ada_2, norm1_g_2, norm2_g_2, w_in_2, lb_logits_2, rec_out_g_2,
        q_norm_g_2, k_norm_g_2, idx_k_norm_g_2, idx_k_norm_b_2, attn_out_g_2, rel_bias_2,
        w_out_2, w_rg_2, b_rg_2, w_re_2, b_re_2, w1_2, w3_2, w2_2,
    )


_drawn_inputs = setup_inputs


def setup_inputs(seed=0):
    import zlib

    import numpy as np

    out = dict(_drawn_inputs(seed))
    spreads = {}
    factors = {'b_merge': 2.964,
     'rg_b': 6.037,
     'norm1_g_2': 3.137,
     'norm2_g_2': 8.0,
     'lb_logits_2': 8.0,
     'rec_out_g_2': 8.0,
     'q_norm_g_2': 8.0,
     'k_norm_g_2': 8.0,
     'idx_k_norm_g_2': 3.952,
     'idx_k_norm_b_2': 4.735,
     'attn_out_g_2': 8.0,
     'b_rg_2': 8.0,
     'b_re_2': 42.444}
    for name, (base, spread) in spreads.items():
        noise = np.random.default_rng([zlib.crc32(name.encode()), seed]).standard_normal(out[name].shape)
        drawn = base * np.exp(spread * noise) if base else spread * noise
        out[name] = __import__('jax').numpy.asarray(drawn.astype(out[name].dtype))
    for name, factor in factors.items():
        out[name] = (out[name] * factor).astype(out[name].dtype)
    return out
```

```python
from contextlib import ExitStack

import numpy as np

import concourse.bass as bass
from concourse import mybir

F32 = mybir.dt.float32
F32R = mybir.dt.float32r
U8 = mybir.dt.uint8
ALU = mybir.AluOpType
ACT = mybir.ActivationFunctionType
AX_X = mybir.AxisListType.X
AX_XY = mybir.AxisListType.XY

P = 128
T = 256
TT = T // P
D = 1024
KD = D // P
DEPTH = 2
D_FF = 2816
FFN_STEPS = D_FF // 256
HEADS = 4
LN_EPS = 1e-5
RMS_EPS = 1e-6
ALPHA = (2.0 * DEPTH) ** 0.25
RING = 3
UNIT = 2048
UNITS_FFN = 3 * FFN_STEPS
UNITS_HALF = 15
UNITS_MERGE = 12
OFF_MIX = UNITS_FFN
OFF_MERGE = OFF_MIX + 2 * UNITS_HALF
OFF_FFN2 = OFF_MERGE + UNITS_MERGE
UNITS_LAYER = OFF_FFN2 + UNITS_FFN
assert UNITS_LAYER % RING == 0 and UNITS_HALF % RING == 0
ROUNDS_LAYER = UNITS_LAYER // RING
ROUND_2 = DEPTH * ROUNDS_LAYER
EXPERTS = 16
MOE_STEPS = 2 * EXPERTS
OFF_WOUT2 = 16
OFF_MOE = 20
UNITS = DEPTH * UNITS_LAYER + OFF_MOE + 3 * MOE_STEPS
V_SC, V_RC, V_RCB, V_BM, V_RGB, V_A, NVEC = 0, 3, 7, 8, 10, 12, 13
PROJ = {"x_r": 3 * D, "y_r": 4 * D, "c_gate": D, "v": 2 * D, "b_gate": 0, "g_a": 5 * D, "g_b": 6 * D}
HALF = [("x_r", 0), ("x_r", 1), ("y_r", 0), ("y_r", 1), ("gates", None)] + [
    (name, a) for a in range(2) for name in ("c_gate", "v", "b_gate", "g_a", "g_b")]
PROJ_UNITS = [u for u in HALF if u[0] != "gates"]
BANK_USES = [len(PROJ_UNITS[b::4]) for b in range(4)]
MERGE = [("conv", 0), ("conv", 1), ("conv", 2), ("conv", 3), ("rnn", 0), ("rnn", 1), ("wo", 0), ("rnn", 2),
         ("wo", 1), ("rnn", 3), ("wo", 2), ("wo", 3)]
NCONST = 6 * DEPTH + 2
IN2_COLS = [0, 256, 512, 768, 1536, 1792, 1024, 1280, 2048, 2304, 2560, 2816, 3072, 3328, 3584, 3840]
BLOCK2_LOADS = 9
TOPK = 64
BIG = 3.0e38
TAKEN = 3.3e38
A_HEADS = 8
A_DH = 64
LEVELS = 8
HANK = 384


def constants():
    rel = np.arange(HANK) - 255
    far = np.maximum(np.abs(rel), 1).astype(np.float32)
    large = 8 + (np.log(far / np.float32(8)) / np.float32(np.log(16)) * np.float32(8)).astype(np.int32)
    bucket = np.where(rel > 0, 16, 0) + np.where(np.abs(rel) < 8, np.abs(rel), np.minimum(large, 15))
    onehot = (bucket[None, :] == np.arange(32)[:, None]).astype(np.float32)
    s, t = np.arange(P)[:, None], np.arange(P)[None, :]
    masks = [s == t] + [(s // (2 * h) == t // (2 * h)) & (s % (2 * h) < h) & (t % (2 * h) >= h)
                        for h in (1, 2, 4, 8, 16, 32, 64)]
    levels = np.stack(masks, 1).astype(np.float32)
    eye = np.eye(P, dtype=np.float32)
    return {"c_onehot": onehot, "c_levels": levels, "c_eye": eye, "c_flip": np.ascontiguousarray(eye[::-1])}


def cols(w, col):
    return w[:, col:col + 256].reshape(KD, P, 256).transpose(1, 0, 2).reshape(P, UNIT)


def rows(w, row):
    return w[row:row + 256].reshape(2, P, D).transpose(1, 0, 2).reshape(P, UNIT)


def swiglu_units(steps):
    steps = list(steps)
    order = list(steps[0][:2])
    for before, (g, u, _) in zip(steps, steps[1:]):
        order += [g, u, before[2]]
    return order + [steps[-1][2]]


def weight_stream(a):
    units = []

    def ffn(l, f):
        w1, w2 = a["ffn_w1"][l, f], a["ffn_w2"][l, f]
        return swiglu_units((cols(w1, c), cols(w1, D_FF + c), rows(w2, c)) for c in range(0, D_FF, 256))

    for l in range(DEPTH):
        units += ffn(l, 0)
        for hf in range(2):
            rg = a["rg_w"][l][:, 2 * hf:2 * hf + 2].reshape(2, 2, 2, P, 256)
            units += [rg.transpose(3, 0, 1, 2, 4).reshape(P, UNIT) if name == "gates"
                      else cols(a["w_in"][l], PROJ[name] + 256 * (2 * hf + head)) for name, head in HALF]
        w = {"conv": a["w_out_conv"][l], "rnn": a["w_out_rnn"][l]}
        units += [rows(a["w_o"][l], 256 * q) if kind == "wo" else cols(w[kind], 256 * q) for kind, q in MERGE]
        units += ffn(l, 1)
    units += [cols(a["w_in_2"][0], c) for c in IN2_COLS]
    units += [rows(a["w_out_2"][0], 256 * q) for q in range(4)]
    w1, w3, w2 = a["w1_2"][0], a["w3_2"][0], a["w2_2"][0]
    units += swiglu_units((cols(w1[e], c), cols(w3[e], c), rows(w2[e], c)) for e in range(EXPERTS) for c in (0, 256))
    assert len(units) == UNITS
    ada, pieces = a["w_ada_2"][0].reshape(KD, P, 6 * D), []
    for c in (0, 3 * D):
        for k in range(0, KD, 2):
            pieces += [ada[k, :, c:c + 2 * D], ada[k + 1, :, c:c + 2 * D],
                       np.concatenate([ada[k, :, c + 2 * D:c + 3 * D], ada[k + 1, :, c + 2 * D:c + 3 * D]], 1)]
    return np.stack(units), np.stack(pieces)


def at(base_round, offset):
    return base_round + offset // RING, offset % RING


def build(nc, t, out):
    ctx = ExitStack()
    with ctx:
        def sb(name, shape, dt=F32, scope=ctx):
            return scope.enter_context(nc.sbuf_tensor(name, shape, dt))

        def sem(name):
            return ctx.enter_context(nc.semaphore(name))

        raw = sb("raw", [P, RING, UNIT])
        whi = sb("whi", [P, RING, UNIT], F32R)
        wlo = sb("wlo", [P, RING, UNIT], F32R)
        x = sb("x_sb", [P, TT, D])
        xThi = sb("xThi", [P, KD, T], F32R)
        xTlo = sb("xTlo", [P, KD, T], F32R)
        lnrow = sb("lnrow", [P, 2, D])
        mod = sb("mod", [P, 6 * D])
        eye = sb("eye", [P, P])
        zero_w = sb("zero_w", [P, P], F32R)
        ones = sb("ones", [P, P])
        vrows = sb("vrows", [NVEC * KD, DEPTH, P])
        crows = sb("crows", [2 * KD, P])
        tick = sb("tick", [P, 1])
        spare = sb("spare", [P, 1])
        stats = sb("stats", [P, TT, 2, 6])
        mv = sb("mv", [P, TT, 2])
        std = sb("std", [P, TT, 1])
        rstd = sb("rstd", [P, TT, 1])
        var = sb("var", [P, TT, 1])
        newt = sb("newt", [P, 32])
        eps = sb("eps", [P, 2])
        vecs = sb("vecs", [P, DEPTH, NVEC, 2, 4])
        now = sb("now", [P, NVEC, 4])
        spt = sb("spt", [P, 5, DEPTH * KD])
        cvec = sb("cvec", [P, 2, KD])
        csil = sb("csil", [P, KD])
        lbt = sb("lbt", [P, 6, HEADS])
        ps = ctx.enter_context(nc.psum_tensor("ps", [P, 8 * 512], F32))

        def bank(b, a=0, e=512):
            return ps[:, b * 512 + a:b * 512 + e]

        def banks(b, n):
            return ps[:, b * 512:(b + n) * 512]

        def halves(b, n=1):
            return banks(b, n).rearrange("p (c t) -> p c t", t=T)

        def xT_banks(i):
            return banks(2 * i, 2).rearrange("p (k t) -> p k t", t=P)

        ffn_scope = ExitStack()
        sil = sb("sil", [P, 2, T], F32, ffn_scope)
        hid = sb("hid", [P, 2, 2, T], F32, ffn_scope)
        hhi = sb("hhi", [P, 2, 2, T], F32R, ffn_scope)
        hlo = sb("hlo", [P, 2, 2, T], F32R, ffn_scope)
        moe_scope = ExitStack()
        cmb = sb("cmb", [P, EXPERTS, T], F32, moe_scope)
        moe_scope.close()
        ffn_scope.close()

        mix_scope = ExitStack()
        zpad = sb("zpad", [P, 2, 2 + T], F32, mix_scope)
        xrp = sb("xrp", [P, 2, 3 + T], F32, mix_scope)
        cv = sb("cv", [P, 2, T], F32, mix_scope)
        gin = sb("gin", [P, 4, T], F32, mix_scope)
        ga = sb("ga", [P, KD, T], F32, mix_scope)
        gb = sb("gb", [P, KD, T], F32, mix_scope)
        yahi = sb("yahi", [P, KD, T], F32R, mix_scope)
        yalo = sb("yalo", [P, KD, T], F32R, mix_scope)
        ybhi = sb("ybhi", [P, KD, T], F32R, mix_scope)
        yblo = sb("yblo", [P, KD, T], F32R, mix_scope)
        head_scope = ExitStack()
        xc = sb("xc", [P, 4, T], F32, head_scope)
        gel = sb("gel", [P, 4, T], F32, head_scope)
        split_scope = ExitStack()
        xchi = sb("xchi", [P, 4, T], F32R, split_scope)
        xclo = sb("xclo", [P, 4, T], F32R, split_scope)
        split_scope.close()
        gate_scope = ExitStack()
        tt_ = sb("tt_", [P, 4, T], F32, gate_scope)
        rr = sb("rr", [P, 4, T], F32, gate_scope)
        gate_scope.close()
        head_scope.close()
        adaraw = sb("adaraw", [P, 2, UNIT], F32, mix_scope)
        mix_scope.close()

        b2 = ExitStack()
        vtok = sb("vtok", [P, TT, 512], F32, b2)
        gate = sb("gate", [P, TT, 512], F32, b2)
        qk = sb("qk", [P, TT, 1024], F32, b2)
        av = sb("av", [P, TT, 512], F32, b2)
        iqT = sb("iqT", [P, 4, T], F32, b2)
        ikT = sb("ikT", [P, T], F32, b2)
        ikd = sb("ikd", [P, TT, P], F32, b2)
        cat = sb("cat", [P, TT, D], F32, b2)
        outg = sb("outg", [P, 1024], F32, b2)
        qkg = sb("qkg", [P, 4, A_DH], F32, b2)
        small = sb("small", [P, KD, 72], F32, b2)
        iw = sb("iw", [P, TT, 8], F32, b2)
        nrm = sb("nrm", [P, 4, 32], F32, b2)
        top8 = sb("top8", [P, 8], F32, b2)
        flip = sb("flip", [P, P], F32, b2)
        rec_scope = ExitStack()
        levels = sb("levels", [P, LEVELS, P], U8, rec_scope)
        qT = sb("qT", [P, HEADS, T], F32, rec_scope)
        fT = sb("fT", [P, HEADS, T], F32, rec_scope)
        kT = sb("kT", [P, HEADS, T], F32, rec_scope)
        suf = sb("suf", [P, HEADS, T], F32, rec_scope)
        qdT = sb("qdT", [P, HEADS, T], F32, rec_scope)
        kdT = sb("kdT", [P, HEADS, T], F32, rec_scope)
        amat = sb("amat", [P, 2 * HEADS, P], F32, rec_scope)
        across = sb("across", [P, HEADS, P], F32, rec_scope)
        rec_scope.close()
        att_scope = ExitStack()
        score = sb("score", [P, 2, T], F32, att_scope)
        hank = sb("hank", [P, A_HEADS, T], F32, att_scope)
        qkT = sb("qkT", [P, 8, T], F32, att_scope)
        lg = sb("lg", [P, A_HEADS, T], F32, att_scope)
        table = sb("table", [32, HANK + A_HEADS], F32, att_scope)
        relv = sb("relv", [A_HEADS, HANK], F32, att_scope)
        pT = qk[:, :, :].rearrange("p k (h t) -> p k h t", h=A_HEADS)
        att_scope.close()
        b2.close()
        route = ExitStack()
        rpad = sb("rpad", [P, 9216], F32, route)
        del rpad
        rw = sb("rw", [P, KD, 20], F32, route)
        rbias = sb("rbias", [P, 20], F32, route)
        rlog = sb("rlog", [P, TT, 20], F32, route)
        rt = sb("rt", [P, TT, 64], F32, route)
        comb = sb("comb", [P, TT, EXPERTS], F32, route)
        route.close()
        scratch = t["scratch"]

        loaded = [sem(f"loaded{s}") for s in range(RING)]
        hi_done = sem("hi_done")
        lo_done = sem("lo_done")
        used = sem("used")
        const_in = sem("const_in")
        bada_in = sem("bada_in")
        rows_in = sem("rows_in")
        rows_free = sem("rows_free")
        setup_dve = sem("setup_dve")
        setup_act = sem("setup_act")
        setup_pe = sem("setup_pe")
        x_in = sem("x_in")
        eye_in = sem("eye_in")
        y0_done = sem("y0_done")
        silu_done = sem("silu_done")
        hid_done = sem("hid_done")
        hhi_done = sem("hhi_done")
        hlo_done = sem("hlo_done")
        mv_done = sem("mv_done")
        std_done = sem("std_done")
        x_done = sem("x_done")
        xT_ps = sem("xT_ps")
        xThi_done = sem("xThi_done")
        xTlo_done = sem("xTlo_done")
        half_start = sem("half_start")
        bank_free = [sem(f"bank_free{b}") for b in range(4)]
        xr_done = sem("xr_done")
        xc_part = sem("xc_part")
        xc_done = sem("xc_done")
        xchi_done = sem("xchi_done")
        xclo_done = sem("xclo_done")
        cg_done = sem("cg_done")
        z_done = sem("z_done")
        cv_part = sem("cv_part")
        cv_done = sem("cv_done")
        yahi_done = sem("yahi_done")
        yalo_done = sem("yalo_done")
        gates_read = sem("gates_read")
        t_done = sem("t_done")
        t_read = sem("t_read")
        sqrt_done = sem("sqrt_done")
        yb_done = sem("yb_done")
        ybhi_done = sem("ybhi_done")
        yblo_done = sem("yblo_done")
        merged = sem("merged")
        m_done = sem("m_done")
        mhi_done = sem("mhi_done")
        mlo_done = sem("mlo_done")
        ada_in = [sem("ada_in0"), sem("ada_in1")]
        ada_used = sem("ada_used")
        ev = {name: sem(name) for name in (
            "mod0_ps mod1_ps mod2_ps mod0 mod1 mod2 "
            "gain1_in block2_in gain2_in table_in hank_in router_in rel_out "
            "ss1 std1 ss2 std2 h1_free "
            "cat_rec evac lvl_ready lvl_ps rec_in recv_ps rec_sq rec_ss rec_std rec_free "
            "ik_ps ik_mv ik_std ik_norm ikT_ps ikT qk_sq qk_ss qk_std qk_norm qkT_ps qkT "
            "rel_ps rel sc0_ps sc1_ps relu0 relu1 score0 lg0_ps lg1_ps lg0 lg1 exp0 exp1 lg_ps0 lg_ps1 "
            "lg_sum0 lg_sum1 pT0 pT1 av0_ps av1_ps araw att_sq att_ss att_std att_done "
            "route_ps rexp_in rexp rexp2_in rexp2 comb comb_ps comb_lo comb_hi final").split()}
        out_done = sem("out_done")


        BASE = ROUND_2
        N_H1, N_CAT, N_H2 = 3 * DEPTH + 1, 3 * DEPTH + 2, 3 * DEPTH + 3
        EVAC_HOLD = 4
        hilo = [xTlo[:, :, :].bitcast(F32), xThi[:, :, :].bitcast(F32)]
        SPAN = [P, T]

        def by_half(m, h):
            return m[:, :, :].rearrange("p a t -> p (a t)").rearrange("p (b two s) -> p b two s", two=2, s=h)

        def row(m, n):
            return m[:, n * D:(n + 1) * D]

        def sp_block2(sp):
            for i in range(TT):
                sp.wait_ge(ev["final"], i + 1)
                sp.dma_start(out[0, i * P:(i + 1) * P, :], x[:, i, :]).then_inc(out_done, 16)
            sp.wait_ge(out_done, 32)

        def pool_block2(pool):
            pool.wait_ge(rows_free, 3 * DEPTH + 1)
            pool.dma_start(lnrow[:, 0, :], t["norm1_g_2"].partition_broadcast(P)).then_inc(ev["gain1_in"], 16)
            loads = [(amat[:, :, :], t["c_levels"]), (flip[:, :], t["c_flip"]),
                     (outg[:, 0:512], t["rec_out_g_2"].partition_broadcast(P)),
                     (outg[:, 512:], t["attn_out_g_2"].partition_broadcast(P)),
                     (small[:, :, :], t["w_in_2"].rearrange("o (k p) n -> p (o k) n", p=P)[:, :, 4096:4168])]
            loads += [(qkg[:, n, :], t[name].partition_broadcast(P)) for n, name in
                      enumerate(("q_norm_g_2", "k_norm_g_2", "idx_k_norm_g_2", "idx_k_norm_b_2"))]
            assert len(loads) == BLOCK2_LOADS
            for dst, src in loads:
                pool.dma_start(dst, src).then_inc(ev["block2_in"], 16)
            pool.wait_ge(ev["h1_free"], 1)
            pool.dma_start(lnrow[:, 0, :], t["norm2_g_2"].partition_broadcast(P)).then_inc(ev["gain2_in"], 16)
            pool.wait_ge(ev["rec_free"], 1)
            pool.dma_start(table[:, 0:HANK], t["c_onehot"]).then_inc(ev["table_in"], 16)
            pool.dma_start(table[:, HANK:], t["rel_bias_2"]).then_inc(ev["table_in"], 16)
            pool.wait_ge(ev["rel_out"], 16)
            sc = t["scratch"]
            pool.dma_start(hank[:, :, :], bass.AP(tensor=sc.tensor, offset=sc.offset, ap=[[1, P], [HANK, A_HEADS], [1, T]])
                           ).then_inc(ev["hank_in"], 16)
            pool.wait_ge(x_done, 2 * N_CAT + 2)
            pool.dma_start(rw[:, :, 0:4], t["w_rg_2"].rearrange("o (k p) n -> p (o k) n", p=P)).then_inc(ev["router_in"], 16)
            pool.dma_start(rw[:, :, 4:20], t["w_re_2"].rearrange("o (k p) n -> p (o k) n", p=P)).then_inc(ev["router_in"], 16)
            pool.dma_start(rbias[:, 0:4], t["b_rg_2"].partition_broadcast(P)).then_inc(ev["router_in"], 16)
            pool.dma_start(rbias[:, 4:20], t["b_re_2"].partition_broadcast(P)).then_inc(ev["router_in"], 16)

        def pe_block2(pe, cols_unit, tokens_unit, rows_unit, transpose_x, open_sums):
            mm = nc.tensor.matmul

            def mod_sums(r, b):
                for c in range(4):
                    last = mm(bank(b + c), ones[:, :], mod[:, r * 2048 + c * 512:r * 2048 + (c + 1) * 512],
                              start=True, stop=True)
                last.then_inc(ev[f"mod{r}_ps"], 1)

            pe.wait_ge(x_done, 6 * DEPTH + 2)
            mod_sums(0, 4)
            pe.wait_ge(xTlo_done, 12 * DEPTH + 4)
            mod_sums(1, 0)
            pe.wait_ge(ev["mod0"], 1)
            mod_sums(2, 4)
            pe.wait_ge(ev["mod1"], 1)
            transpose_x(N_H1, cat)
            pe.wait_ge(xTlo_done, 4 * N_H1 + 4)

            def level(n):
                pe.wait_ge(ev["lvl_ready"], n + 1)
                b = 4 + 2 * (n % 2)
                k, q = (kT, qT) if n == 0 else (kdT, qdT)
                if n == 0:
                    pe.wait_ge(ev["mod2"], 1)
                for head in range(HEADS):
                    if n == LEVELS:
                        last = mm(bank(b, head * P, (head + 1) * P), k[:, head, 0:P], q[:, head, P:T], start=True, stop=True)
                        continue
                    for i in range(TT):
                        c = (head * 2 + i) * P
                        sl = slice(i * P, (i + 1) * P)
                        last = mm(banks(b, 2)[:, c:c + P], k[:, head, sl], q[:, head, sl], start=True, stop=True)
                last.then_inc(ev["lvl_ps"], 1)

            for u in range(16):
                if u >= EVAC_HOLD:
                    pe.wait_ge(ev["evac"], u - EVAC_HOLD + 1)
                b = u % EVAC_HOLD
                if u < 4 or u >= 14:
                    cols_unit(*at(BASE, u), xThi, xTlo, [bank(b, 0, T), bank(b, T)])
                else:
                    tokens_unit(*at(BASE, u), xThi, xTlo, b)
                if 5 <= u < 5 + LEVELS + 1:
                    level(u - 5)
            pe.wait_ge(ev["block2_in"], 16 * BLOCK2_LOADS)
            pe.wait_ge(ev["evac"], 14)
            for i in range(TT):
                for k in range(KD):
                    for part in range(2):
                        last = mm(bank(i, 0, 72), hilo[part][:, k, i * P:(i + 1) * P], small[:, k, :],
                                  start=k == 0 and part == 0, stop=k == KD - 1 and part == 1)
            last.then_inc(ev["ik_ps"], 1)
            pe.wait_ge(ev["rec_in"], 1)
            for head in range(HEADS):
                hs = slice(head * P, (head + 1) * P)
                mm(bank(6)[:, hs], amat[:, 2 * head, :], vtok[:, 0, hs], start=True, stop=True)
                mm(bank(7)[:, hs], amat[:, 2 * head + 1, :], vtok[:, 1, hs], start=True, stop=False)
                last = mm(bank(7)[:, hs], across[:, head, :], vtok[:, 0, hs], start=False, stop=True)
            last.then_inc(ev["recv_ps"], 1)
            pe.wait_ge(ev["ik_norm"], 1)
            for i in range(TT):
                last = nc.tensor.transpose(bank(4, i * P, (i + 1) * P), ikd[:, i, :], eye[:, :])
            last.then_inc(ev["ikT_ps"], 1)
            pe.wait_ge(ev["table_in"], 32)
            mm(ps[0:A_HEADS, 5 * 512:5 * 512 + HANK], table[:, HANK:], table[:, 0:HANK], start=True,
               stop=True).then_inc(ev["rel_ps"], 1)
            pe.wait_ge(ev["qk_norm"], 1)
            pe.wait_ge(ev["evac"], 16)
            for i in range(TT):
                for k in range(8):
                    last = nc.tensor.transpose(xT_banks(i)[:, k, :], qk[:, i, k * P:(k + 1) * P], eye[:, :])
            last.then_inc(ev["qkT_ps"], 1)

            def head_rows(h):
                return slice(64 * (h % 2), 64 * (h % 2) + 64)

            def pos(h):
                return h % 2 * 4 + h // 2

            def spans(i):
                return banks(4 * i, 2 + 2 * i).rearrange("p (h s) -> p h s", s=SPAN[i])

            pe.wait_ge(ev["ikT"], 1)
            pe.wait_ge(ev["qkT"], 1)
            pe.wait_ge(ev["rel"], 1)
            pe.wait_ge(ev["cat_rec"], 1)
            for i in range(TT):
                for h in range(A_HEADS):
                    last = mm(spans(i)[:, pos(h), :], iqT[head_rows(h), h // 2, i * P:(i + 1) * P],
                              ikT[head_rows(h), 0:SPAN[i]], start=True, stop=True)
                last.then_inc(ev[f"sc{i}_ps"], 1)
            pe.wait_ge(ev["hank_in"], 16)
            for i in range(TT):
                pe.wait_ge(ev[f"relu{i}"], 1)
                for h in range(A_HEADS):
                    mm(spans(i)[:, pos(h), :], qkT[head_rows(h), h // 2, i * P:(i + 1) * P],
                       qkT[head_rows(h), 4 + h // 2, 0:SPAN[i]], start=True, stop=False)
                    last = mm(spans(i)[:, pos(h), :], flip[:, :], hank[:, h, T - SPAN[i]:T], start=False, stop=True)
                last.then_inc(ev[f"lg{i}_ps"], 1)
            for i in range(TT):
                pe.wait_ge(ev[f"exp{i}"], 1)
                if i == 1:
                    pe.wait_ge(ev["araw"], 1)
                b = 2 - 2 * i
                lgv = lg[:, :, :].rearrange("p h s -> p (h s)")[:, 0:A_HEADS * SPAN[i]].rearrange(
                    "p (h s) -> p h s", s=SPAN[i])
                for kb in range(i + 1):
                    for h in range(A_HEADS):
                        c = (kb * A_HEADS + h) * P
                        last = nc.tensor.transpose(banks(b, 2 + 2 * i)[:, c:c + P], lgv[:, h, kb * P:(kb + 1) * P], eye[:, :])
                last.then_inc(ev[f"lg_ps{i}"], 1)
                pe.wait_ge(ev[f"pT{i}"], 1)
                b = 2 + 2 * i
                for h in range(A_HEADS):
                    for kb in range(i + 1):
                        last = mm(bank(b, pos(h) * A_DH, (pos(h) + 1) * A_DH), pT[:, kb, pos(h), :], av[:, kb, h * A_DH:(h + 1) * A_DH],
                                  start=kb == 0, stop=kb == i)
                last.then_inc(ev[f"av{i}_ps"], 1)
            transpose_x(N_CAT, cat)
            pe.wait_ge(xTlo_done, 4 * N_CAT + 4)
            for q in range(4):
                rows_unit(*at(BASE, OFF_WOUT2 + q), xThi[:, 2 * q:2 * q + 2], xTlo[:, 2 * q:2 * q + 2], q == 0, q == 3)
            transpose_x(N_H2, cat)
            pe.wait_ge(xTlo_done, 4 * N_H2 + 4)
            pe.wait_ge(ev["router_in"], 64)
            for i in range(TT):
                for k in range(KD):
                    for part in range(2):
                        last = mm(bank(4 + i, 0, 20), hilo[part][:, k, i * P:(i + 1) * P], rw[:, k, :],
                                  start=k == 0 and part == 0, stop=k == KD - 1 and part == 1)
            last.then_inc(ev["route_ps"], 1)
            pe.wait_ge(ev["comb"], 1)
            for e in range(EXPERTS):
                for i in range(TT):
                    c = e * T + i * P
                    last = mm(ps[:, c:c + P], comb[:, i, e:e + 1].to_broadcast([P, P]), eye[:, :], start=True, stop=True)
            last.then_inc(ev["comb_ps"], 1)
            pe.wait_ge(ev["comb_lo"], 1)
            pe.wait_ge(ev["comb_hi"], 1)
            count = DEPTH * 2 * FFN_STEPS
            open_sums()

            def gate_up(base, o, par):
                cols_unit(*at(base, o), xThi, xTlo, [bank(2 * par, 0, T), bank(2 * par + 1, 0, T)])
                cols_unit(*at(base, o + 1), xThi, xTlo, [bank(2 * par, T), bank(2 * par + 1, T)])

            gate_up(BASE, OFF_MOE, 0)
            with pe.Fori(0, EXPERTS - 1) as i:
                for s in range(2):
                    o = OFF_MOE + 2 + 3 * s
                    gate_up(BASE + 2 * i, o, 1 - s)
                    pe.wait_ge(hlo_done, 2 * i + (count + s + 1))
                    rows_unit(*at(BASE + 2 * i, o + 2), hhi[:, s], hlo[:, s], False, False)
            o = OFF_MOE + 3 * MOE_STEPS - 4
            gate_up(BASE, o, 1)
            pe.wait_ge(hlo_done, count + MOE_STEPS - 1)
            rows_unit(*at(BASE, o + 2), hhi[:, 0], hlo[:, 0], False, False)
            pe.wait_ge(hlo_done, count + MOE_STEPS)
            rows_unit(*at(BASE, o + 3), hhi[:, 1], hlo[:, 1], False, True)

        def act_block2(act, turn, split_xT, silu, hid_hi):
            act_fn = nc.scalar.activation

            def rms_root(name):
                act.wait_ge(ev[f"ss{name}"], 1)
                act_fn(std[:, :, 0], var[:, :, 0], ACT.Sqrt).then_inc(ev[f"std{name}"], 1)

            rms_root("1")
            act.wait_ge(ev["mod0_ps"], 1)
            act_fn(mod[:, 0:2048], banks(4, 4), ACT.Copy).then_inc(ev["mod0"], 1)
            act.wait_ge(ev["mod2_ps"], 1)
            act_fn(mod[:, 4096:6144], banks(4, 4), ACT.Copy).then_inc(ev["mod2"], 1)
            split_xT(N_H1)
            for u in range(16):
                turn(BASE, u)
                src = halves(u % EVAC_HOLD)
                c = u % 2
                cs = slice(c * T, (c + 1) * T)
                if u < 2:
                    ins = act_fn(qT[:, 2 * c:2 * c + 2, :], src, ACT.Silu)
                elif u < 4:
                    ins = act_fn(fT[:, 2 * c:2 * c + 2, :], src, ACT.Tanh, scale=0.5)
                elif u < 6:
                    ins = act_fn(gate[:, :, cs], src, ACT.Silu)
                elif u < 8:
                    ins = act_fn(vtok[:, :, cs], src, ACT.Copy)
                elif u < 12:
                    o = (u - 8) * T
                    ins = act_fn(qk[:, :, o:o + T], src, ACT.Copy)
                elif u < 14:
                    ins = act_fn(av[:, :, cs], src, ACT.Copy)
                else:
                    ins = act_fn(iqT[:, 2 * c:2 * c + 2, :], src, ACT.Copy)
                ins.then_inc(ev["evac"], 1)

            def root(dst, src, count, n, event):
                act_fn(nrm[:, dst, 0:count], nrm[:, src, 0:count], ACT.Sqrt, bias=eps[:, 1:2],
                       scale=1.0 / n).then_inc(ev[event], 1)

            act.wait_ge(ev["recv_ps"], 1)
            act_fn(qdT[:, :, :].rearrange("p a t -> p (a t)"), banks(6, 2), ACT.Square).then_inc(ev["rec_sq"], 1)
            act.wait_ge(ev["ik_mv"], 1)
            act_fn(std[:, :, 0], mv[:, :, 1], ACT.Sqrt, bias=eps[:, 1:2]).then_inc(ev["ik_std"], 1)
            act.wait_ge(ev["rec_ss"], 1)
            root(1, 0, 8, P, "rec_std")
            act.wait_ge(ev["rec_free"], 1)
            act_fn(lg[:, :, :].rearrange("p h s -> p (h s)"), qk[:, :, :].rearrange("p i c -> p (i c)"),
                   ACT.Square).then_inc(ev["qk_sq"], 1)
            act.wait_ge(ev["ikT_ps"], 1)
            act_fn(ikT[:, :], bank(4, 0, T), ACT.Copy).then_inc(ev["ikT"], 1)
            act.wait_ge(ev["qk_ss"], 1)
            root(1, 0, 32, A_DH, "qk_std")
            act.wait_ge(ev["rel_ps"], 1)
            act_fn(relv[:, :], ps[0:A_HEADS, 5 * 512:5 * 512 + HANK], ACT.Copy).then_inc(ev["rel"], 1)
            act.wait_ge(ev["rel"], 1)
            act.dma_start(t["scratch"], relv[:, :]).then_inc(ev["rel_out"], 16)
            act.wait_ge(ev["qkT_ps"], 1)
            for i in range(TT):
                ins = act_fn(qkT[:, :, i * P:(i + 1) * P], xT_banks(i), ACT.Copy)
            ins.then_inc(ev["qkT"], 1)
            lgf = lg[:, :, :].rearrange("p h s -> p (h s)")
            for i in range(TT):
                act.wait_ge(ev[f"sc{i}_ps"], 1)
                if i == 1:
                    act.wait_ge(ev["score0"], 1)
                act_fn(lgf[:, 0:A_HEADS * SPAN[i]], banks(4 * i, 2 + 2 * i), ACT.Relu).then_inc(ev[f"relu{i}"], 1)
            for i in range(TT):
                part = lgf[:, 0:A_HEADS * SPAN[i]]
                act.wait_ge(ev[f"lg{i}"], 1)
                act_fn(part, part, ACT.Exp).then_inc(ev[f"exp{i}"], 1)
                act.wait_ge(ev[f"lg_ps{i}"], 1)
                act_fn(pT[:, 0:i + 1].rearrange("p k h t -> p (k h t)"), banks(2 - 2 * i, 2 + 2 * i),
                       ACT.Copy).then_inc(ev[f"pT{i}"], 1)
            act.wait_ge(ev["araw"], 2)
            act_fn(lgf[:, 0:1024].rearrange("p (i c) -> p i c", i=TT), cat[:, :, 512:], ACT.Square).then_inc(ev["att_sq"], 1)
            act.wait_ge(ev["att_ss"], 1)
            root(1, 0, 16, A_DH, "att_std")
            split_xT(N_CAT)
            for q in range(3):
                turn(BASE, OFF_WOUT2 + q)
            rms_root("2")
            split_xT(N_H2)
            turn(BASE, OFF_WOUT2 + 3)
            act.wait_ge(ev["rexp_in"], 1)
            act_fn(rt[:, :, 8:12], rt[:, :, 8:12], ACT.Exp).then_inc(ev["rexp"], 1)
            act.wait_ge(ev["rexp2_in"], 1)
            act_fn(rt[:, :, 32:33], rt[:, :, 32:33], ACT.Exp).then_inc(ev["rexp2"], 1)
            act.wait_ge(ev["comb_ps"], 1)
            act_fn(cmb[:, 0:8, :].rearrange("p e t -> p (e t)"), banks(0, 4), ACT.Copy).then_inc(ev["comb_lo"], 1)
            count = DEPTH * 2 * FFN_STEPS
            turn(BASE, OFF_MOE)
            silu(0, BASE, OFF_MOE + 1)
            hid_hi(0, count + 1)
            turn(BASE, OFF_MOE + 1)
            with act.Fori(0, EXPERTS - 1) as i:
                for s in range(2):
                    o, par = OFF_MOE + 2 + 3 * s, 1 - s
                    turn(BASE + 2 * i, o)
                    silu(par, BASE + 2 * i, o + 1)
                    hid_hi(par, 2 * i + (count + s + 2))
                    turn(BASE + 2 * i, o + 1)
                    turn(BASE + 2 * i, o + 2)
            last = UNITS - ROUND_2 * RING
            turn(BASE, last - 4)
            silu(1, BASE, last - 3)
            hid_hi(1, count + MOE_STEPS)

        def dve_block2(dve, turn, split_xT, hid_lo, refine):
            v = nc.vector

            def gain(r):
                v.tensor_scalar(lnrow[:, 1, :], row(mod, r), 1.0, None, ALU.add)

            def head_norms(count, n):
                v.tensor_scalar(nrm[:, 3, 0:count], nrm[:, 0, 0:count], 1.0 / n, RMS_EPS, ALU.mult, ALU.add)
                dve.drain()
                refine(nrm[:, 2, 0:count], nrm[:, 1, 0:count], nrm[:, 3, 0:count], newt[:, 0:count])

            def modulate(shift):
                refine(rstd[:, :, 0], std[:, :, 0], var[:, :, 0], newt[:, 0:TT])
                for i in range(TT):
                    v.scalar_tensor_tensor(cat[:, i, :], x[:, i, :], rstd[:, i, 0:1], lnrow[:, 0, :], ALU.mult, ALU.mult)
                    dve.drain()
                    v.tensor_tensor(cat[:, i, :], cat[:, i, :], lnrow[:, 1, :], ALU.mult)
                    dve.drain()
                    v.tensor_tensor(cat[:, i, :], cat[:, i, :], row(mod, shift), ALU.add).then_inc(x_done, 1)

            def mean_squares(name):
                for i in range(TT):
                    for n2 in range(2):
                        v.bn_stats(stats[:, i, n2, :], x[:, i, n2 * 512:(n2 + 1) * 512])
                dve.drain()
                for i in range(TT):
                    v.bn_aggr(mv[:, i, :], stats[:, i, :, :].rearrange("p a b -> p (a b)"))
                dve.drain()
                v.tensor_tensor(var[:, :, 0], mv[:, :, 0], mv[:, :, 0], ALU.mult)
                dve.drain()
                v.scalar_tensor_tensor(var[:, :, 0], var[:, :, 0], RMS_EPS, mv[:, :, 1], ALU.add,
                                       ALU.add).then_inc(ev[f"ss{name}"], 1)

            mean_squares("1")
            dve.wait_ge(ev["gain1_in"], 16)
            dve.wait_ge(ev["mod0"], 1)
            gain(1)
            dve.wait_ge(ev["mod1_ps"], 1)
            v.tensor_copy(mod[:, 2048:4096], banks(0, 4)).then_inc(ev["mod1"], 1)
            dve.wait_ge(ev["std1"], 1)
            modulate(0)
            dve.drain()
            v.memset(tick[:, :], 0.0).then_inc(ev["h1_free"], 1)
            split_xT(N_H1)
            for m, val in ((suf, 1.0), (qdT, 0.0), (kdT, 0.0)):
                v.memset(m[:, :, :], val)
            v.tensor_scalar(lbt[:, 3, :], lbt[:, 1, :], -1.0, None, ALU.mult)
            dve.wait_ge(ev["block2_in"], 16 * BLOCK2_LOADS)
            v.tensor_scalar(qkg[:, 0, :], qkg[:, 0, :], A_DH ** -0.5, None, ALU.mult)
            v.tensor_copy(levels[:, :, :], amat[:, :, :])
            dve.drain()
            v.memset(amat[:, :, :], 0.0)
            dve.drain()

            def select(n):
                b = 4 + 2 * (n % 2)
                v.copy_predicated(amat[:, :, :], levels[:, n:n + 1, :].to_broadcast([P, 2 * HEADS, P]),
                                  banks(b, 2).rearrange("p (m t) -> p m t", t=P))

            def decays(n):
                h = 2 ** (n - 1)
                q, k, f, s, qd, kd = (by_half(m, h) for m in (qT, kT, fT, suf, qdT, kdT))
                v.tensor_tensor(qd[:, :, 1, :], q[:, :, 1, :], f[:, :, 1, :], ALU.mult)
                v.tensor_tensor(kd[:, :, 0, :], k[:, :, 0, :], s[:, :, 0, :], ALU.mult)
                dve.drain()
                if n == LEVELS:
                    v.memset(tick[:, :], 0.0).then_inc(ev["lvl_ready"], 1)
                    return
                shape = [P, f.shape[1], h]
                v.tensor_tensor(s[:, :, 0, :], s[:, :, 0, :], f[:, :, 1, h - 1:h].to_broadcast(shape),
                                ALU.mult).then_inc(ev["lvl_ready"], 1)
                dve.drain()
                v.tensor_tensor(f[:, :, 1, :], f[:, :, 1, :], f[:, :, 0, h - 1:h].to_broadcast(shape), ALU.mult)
                dve.drain()

            for u in range(16):
                turn(BASE, u)
                n = u - 4
                if n == 0:
                    dve.wait_ge(ev["evac"], 4)
                    for head in range(HEADS):
                        hs = slice(head, head + 1)
                        v.tensor_scalar(kT[:, head, :], fT[:, head, :], lbt[:, 3, hs], lbt[:, 1, hs], ALU.mult, ALU.add)
                    dve.drain()
                    for head in range(HEADS):
                        hs = slice(head, head + 1)
                        ins = v.tensor_scalar(fT[:, head, :], fT[:, head, :], lbt[:, 1, hs], lbt[:, 2, hs], ALU.mult, ALU.add)
                    ins.then_inc(ev["lvl_ready"], 1)
                    dve.drain()
                elif 0 < n <= LEVELS:
                    dve.wait_ge(ev["lvl_ps"], n)
                    select(n - 1)
                    decays(n)
            dve.wait_ge(ev["lvl_ps"], LEVELS + 1)
            v.tensor_copy(across[:, :, :].rearrange("p a t -> p (a t)"), bank(4 + 2 * (LEVELS % 2))).then_inc(ev["rec_in"], 1)
            for i in range(TT):
                ins = v.tensor_tensor(gate[:, i, :], gate[:, i, :], outg[:, 0:512], ALU.mult)
            dve.wait_ge(ev["ik_ps"], 1)
            for i in range(TT):
                v.bn_stats(stats[:, i, 0, :], bank(i, 0, A_DH))
                v.tensor_scalar(iw[:, i, :], bank(i, A_DH, 72), float(np.float32(A_HEADS ** -0.5)), A_DH ** -0.5,
                                ALU.mult, ALU.mult)
            dve.drain()
            for i in range(TT):
                ins = v.bn_aggr(mv[:, i, :], stats[:, i, 0, :])
            ins.then_inc(ev["ik_mv"], 1)
            dve.wait_ge(ev["rec_sq"], 1)
            v.tensor_reduce(nrm[:, 0, 0:8], qdT[:, :, :].rearrange("p a t -> p (a t)").rearrange("p (m c) -> p m c", c=P),
                            AX_X, ALU.add).then_inc(ev["rec_ss"], 1)
            dve.wait_ge(ev["ik_std"], 1)
            v.tensor_scalar(var[:, :, 0], mv[:, :, 1], RMS_EPS, None, ALU.add)
            dve.drain()
            refine(rstd[:, :, 0], std[:, :, 0], var[:, :, 0], newt[:, 0:TT])
            for i in range(TT):
                v.tensor_scalar(ikd[:, i, 0:A_DH], bank(i, 0, A_DH), mv[:, i, 0:1], rstd[:, i, 0:1], ALU.subtract, ALU.mult)
            dve.drain()
            for i in range(TT):
                v.tensor_tensor(ikd[:, i, 0:A_DH], ikd[:, i, 0:A_DH], qkg[:, 2, :], ALU.mult)
            dve.drain()
            for i in range(TT):
                v.tensor_tensor(ikd[:, i, 0:A_DH], ikd[:, i, 0:A_DH], qkg[:, 3, :], ALU.add)
            dve.drain()
            v.tensor_copy(ikd[:, :, A_DH:], ikd[:, :, 0:A_DH]).then_inc(ev["ik_norm"], 1)
            dve.wait_ge(ev["rec_std"], 1)
            head_norms(8, P)
            for i in range(TT):
                v.tensor_tensor(cat[:, i, 0:512].rearrange("p (a c) -> p a c", c=P), bank(6 + i).rearrange("p (a c) -> p a c", c=P),
                                nrm[:, 2, 4 * i:4 * i + 4].unsqueeze(2).to_broadcast([P, HEADS, P]), ALU.mult)
            dve.drain()
            v.tensor_tensor(cat[:, :, 0:512], cat[:, :, 0:512], gate[:, :, :], ALU.mult).then_inc(ev["rec_free"], 1)
            v.memset(tick[:, :], 0.0).then_inc(ev["cat_rec"], 1)
            lgf = lg[:, :, :].rearrange("p h s -> p (h s)")
            dve.wait_ge(ev["qk_sq"], 1)
            v.tensor_reduce(nrm[:, 0, 0:32], lgf.rearrange("p (m c) -> p m c", c=A_DH), AX_X, ALU.add).then_inc(ev["qk_ss"], 1)
            dve.wait_ge(ev["qk_std"], 1)
            head_norms(32, A_DH)
            qkf = qk[:, :, :].rearrange("p i c -> p (i c)").rearrange("p (m c) -> p m c", c=A_DH)
            v.tensor_tensor(qkf, qkf, nrm[:, 2, 0:32].unsqueeze(2).to_broadcast([P, 32, A_DH]), ALU.mult)
            dve.drain()
            for i in range(TT):
                for half in range(2):
                    part = qkf[:, 16 * i + 8 * half:16 * i + 8 * half + 8, :]
                    ins = v.tensor_tensor(part, part, qkg[:, half:half + 1, :].to_broadcast([P, A_HEADS, A_DH]), ALU.mult)
            ins.then_inc(ev["qk_norm"], 1)
            for i in range(TT):
                n = SPAN[i]
                rl = lgf[:, 0:A_HEADS * n].rearrange("p (h s) -> p h s", s=n)
                sc = score[:, i, 0:n]
                dve.wait_ge(ev[f"relu{i}"], 1)
                for odd in range(2):
                    part = rl[:, 4 * odd:4 * odd + 4, :]
                    w = iw[:, i, :].rearrange("p (a b) -> p b a", b=2)[:, odd, :]
                    v.tensor_tensor(part, part, w.unsqueeze(2).to_broadcast([P, 4, n]), ALU.mult)
                dve.drain()
                ins = v.tensor_reduce(sc, rl.rearrange("p (b a) s -> p s a b", b=2), AX_XY, ALU.add)
                if i == 0:
                    ins.then_inc(ev["score0"], 1)
                dve.drain()
                v.memset(score[0:64, i, n - 64:n], -BIG)
                dve.drain()
                for _ in range(TOPK // 8):
                    v.max(top8[:, :], sc)
                    dve.drain()
                    v.match_replace(out=sc, in_to_replace=top8[:, :], in_values=sc, imm_value=-TAKEN)
                    dve.drain()
                v.tensor_scalar(sc, sc, -(BIG + TAKEN) / 2, -1.0e30, ALU.is_gt, ALU.mult)
            for i in range(TT):
                n = SPAN[i]
                lv = lgf[:, 0:A_HEADS * n].rearrange("p (h s) -> p h s", s=n)
                dve.wait_ge(ev[f"lg{i}_ps"], 1)
                dve.drain()
                if i == 1:
                    dve.wait_ge(ev["lg_ps0"], 1)
                v.tensor_tensor(lv, banks(4 * i, 2 + 2 * i).rearrange("p (h s) -> p h s", s=n),
                                score[:, i:i + 1, 0:n].to_broadcast([P, A_HEADS, n]), ALU.add)
                dve.drain()
                v.tensor_reduce(nrm[:, 0, 0:8], lv, AX_X, ALU.max)
                dve.drain()
                v.tensor_tensor(lv, lv, nrm[:, 0, 0:8].unsqueeze(2).to_broadcast([P, A_HEADS, n]),
                                ALU.subtract).then_inc(ev[f"lg{i}"], 1)
                dve.wait_ge(ev[f"exp{i}"], 1)
                v.tensor_reduce(nrm[:, 1, 0:8], lv, AX_X, ALU.add)
                dve.drain()
                v.reciprocal(nrm[:, 2, 0:8], nrm[:, 1, 0:8])
                dve.wait_ge(ev[f"av{i}_ps"], 1)
                dve.drain()
                for odd in range(2):
                    ins = v.tensor_tensor(cat[:, i, 512:].rearrange("p (a b c) -> p b a c", b=2, c=A_DH)[:, odd],
                                          bank(2 + 2 * i, 256 * odd, 256 * odd + 256).rearrange("p (a c) -> p a c", c=A_DH),
                                          nrm[:, 2, 4 * odd:4 * odd + 4].unsqueeze(2).to_broadcast([P, 4, A_DH]), ALU.mult)
                ins.then_inc(ev["araw"], 1)
            dve.wait_ge(ev["att_sq"], 1)
            v.tensor_reduce(nrm[:, 0, 0:16], lgf[:, 0:1024].rearrange("p (m c) -> p m c", c=A_DH), AX_X,
                            ALU.add).then_inc(ev["att_ss"], 1)
            dve.wait_ge(ev["att_std"], 1)
            head_norms(16, A_DH)
            for i in range(TT):
                att = cat[:, i, 512:].rearrange("p (h c) -> p h c", c=A_DH)
                v.tensor_tensor(att, att, nrm[:, 2, 8 * i:8 * i + 8].unsqueeze(2).to_broadcast([P, A_HEADS, A_DH]), ALU.mult)
            dve.drain()
            for i in range(TT):
                v.tensor_tensor(cat[:, i, 512:], cat[:, i, 512:], outg[:, 512:], ALU.mult).then_inc(x_done, 1)
            split_xT(N_CAT)
            for q in range(3):
                turn(BASE, OFF_WOUT2 + q)
            dve.wait_ge(ev["gain2_in"], 16)
            dve.wait_ge(used, ROUND_2 * RING + OFF_MOE)
            for i in range(TT):
                v.tensor_tensor(cat[:, i, :], banks(4 + 2 * i, 2), row(mod, 2), ALU.mult)
            dve.drain()
            for i in range(TT):
                v.tensor_tensor(x[:, i, :], x[:, i, :], cat[:, i, :], ALU.add)
            dve.drain()
            mean_squares("2")
            dve.wait_ge(ev["std2"], 1)
            gain(4)
            dve.drain()
            modulate(3)
            split_xT(N_H2)
            turn(BASE, OFF_WOUT2 + 3)

            def R(a, b):
                return rt[:, :, a:b]

            def first(eq, seen, dst):
                v.memset(R(seen, seen + 1), 0.0)
                v.tensor_copy(R(seen + 1, seen + 2), R(eq, eq + 1))
                dve.drain()
                for j in (2, 3):
                    v.tensor_tensor(R(seen + j, seen + j + 1), R(seen + j - 1, seen + j), R(eq + j - 1, eq + j), ALU.max)
                    dve.drain()
                v.tensor_tensor(R(dst, dst + 4), R(eq, eq + 4), R(seen, seen + 4), ALU.is_gt)
                dve.drain()

            def four(ap):
                return ap.to_broadcast([P, TT, 4])

            dve.wait_ge(ev["route_ps"], 1)
            for i in range(TT):
                v.tensor_tensor(rlog[:, i, :], bank(4 + i, 0, 20), rbias[:, :], ALU.add)
            dve.drain()
            v.tensor_reduce(R(0, 1), rlog[:, :, 0:4], AX_X, ALU.max)
            dve.drain()
            v.tensor_tensor(R(4, 8), rlog[:, :, 0:4], four(R(0, 1)), ALU.is_equal)
            v.tensor_tensor(R(8, 12), rlog[:, :, 0:4], four(R(0, 1)), ALU.subtract).then_inc(ev["rexp_in"], 1)
            dve.drain()
            first(4, 12, 16)
            el = rlog[:, :, 4:20].rearrange("p i (g j) -> p i g j", j=4)
            tmp = R(36, 52).rearrange("p i (g j) -> p i g j", j=4)
            v.tensor_tensor(tmp, el, R(16, 20).unsqueeze(3).to_broadcast([P, TT, 4, 4]), ALU.mult)
            dve.drain()
            v.tensor_reduce(R(20, 24), tmp.rearrange("p i g j -> p i j g"), AX_X, ALU.add)
            dve.drain()
            v.tensor_reduce(R(1, 2), R(20, 24), AX_X, ALU.max)
            dve.drain()
            v.tensor_tensor(R(4, 8), R(20, 24), four(R(1, 2)), ALU.is_equal)
            dve.drain()
            first(4, 12, 24)
            v.tensor_scalar(R(52, 56), R(24, 28), -1.0e38, None, ALU.mult)
            dve.drain()
            v.tensor_tensor(R(20, 24), R(20, 24), R(52, 56), ALU.add)
            dve.drain()
            v.tensor_reduce(R(2, 3), R(20, 24), AX_X, ALU.max)
            dve.drain()
            v.tensor_tensor(R(32, 33), R(2, 3), R(1, 2), ALU.subtract).then_inc(ev["rexp2_in"], 1)
            v.tensor_tensor(R(4, 8), R(20, 24), four(R(2, 3)), ALU.is_equal)
            dve.drain()
            first(4, 12, 28)
            dve.wait_ge(ev["rexp"], 1)
            v.tensor_reduce(R(3, 4), R(8, 12), AX_X, ALU.add)
            dve.wait_ge(ev["rexp2"], 1)
            v.tensor_scalar(R(33, 34), R(32, 33), 1.0, None, ALU.add)
            dve.drain()
            v.reciprocal(R(3, 4), R(3, 4))
            v.reciprocal(R(33, 34), R(33, 34))
            dve.drain()
            v.tensor_tensor(R(34, 35), R(32, 33), R(33, 34), ALU.mult)
            dve.drain()
            v.tensor_tensor(R(33, 35), R(33, 35), R(3, 4).to_broadcast([P, TT, 2]), ALU.mult)
            dve.drain()
            v.tensor_tensor(R(24, 28), R(24, 28), four(R(33, 34)), ALU.mult)
            v.tensor_tensor(R(28, 32), R(28, 32), four(R(34, 35)), ALU.mult)
            dve.drain()
            v.tensor_tensor(R(24, 28), R(24, 28), R(28, 32), ALU.add)
            dve.drain()
            for g in range(4):
                ins = v.tensor_tensor(comb[:, :, 4 * g:4 * g + 4], R(24, 28), four(R(16 + g, 17 + g)), ALU.mult)
            ins.then_inc(ev["comb"], 1)
            dve.wait_ge(ev["comb_ps"], 1)
            v.tensor_copy(cmb[:, 8:16, :].rearrange("p e t -> p (e t)"), banks(4, 4)).then_inc(ev["comb_hi"], 1)
            count = DEPTH * 2 * FFN_STEPS

            def hidden(par, expert, n):
                dve.wait_ge(silu_done, n)
                v.tensor_tensor(sil[:, :, :], sil[:, :, :], cmb[:, bass.ds(expert, 1), :].to_broadcast([P, 2, T]), ALU.mult)
                dve.drain()
                up = banks(2 * par, 2).rearrange("p (c u t) -> p c u t", u=2, t=T)[:, :, 1, :]
                v.tensor_tensor(hid[:, par], sil[:, :, :], up, ALU.mult).then_inc(hid_done, 1)

            turn(BASE, OFF_MOE)
            hidden(0, 0, count + 1)
            hid_lo(0, count + 1)
            turn(BASE, OFF_MOE + 1)
            with dve.Fori(0, EXPERTS - 1) as i:
                for s in range(2):
                    o, par = OFF_MOE + 2 + 3 * s, 1 - s
                    turn(BASE + 2 * i, o)
                    hidden(par, i + s, 2 * i + (count + s + 2))
                    hid_lo(par, 2 * i + (count + s + 2))
                    turn(BASE + 2 * i, o + 1)
                    turn(BASE + 2 * i, o + 2)
            turn(BASE, UNITS - ROUND_2 * RING - 4)
            hidden(1, EXPERTS - 1, count + MOE_STEPS)
            hid_lo(1, count + MOE_STEPS)
            dve.wait_ge(used, UNITS)
            for i in range(TT):
                v.tensor_tensor(lnrow[:, i, :], banks(4 + 2 * i, 2), row(mod, 5), ALU.mult)
                dve.drain()
                v.tensor_tensor(x[:, i, :], x[:, i, :], lnrow[:, i, :], ALU.add).then_inc(ev["final"], 1)

        def proj_bank(name, a):
            return PROJ_UNITS.index((name, a)) % 4

        def proj(name, a):
            b = proj_bank(name, a)
            return halves(b), bank_free[b]

        block = ctx.enter_context(nc.Block())

        def unit_no(rnd, slot):
            return rnd * RING + slot

        @block.sync
        def _(sp):
            def load(rnd, slot):
                sp.wait_ge(lo_done, unit_no(rnd, slot) + 1)
                sp.dma_start(raw[:, slot, :], t["stream"][bass.ds(unit_no(rnd, slot), 1), :, :].rearrange(
                    "o p n -> p (o n)")).then_inc(loaded[slot], 16)

            sp.dma_start(eye[:, :], t["c_eye"]).then_inc(eye_in, 16)
            sp.dma_start(x[:, :, :], t["x"].rearrange("o (i p) d -> p (o i) d", p=P)).then_inc(x_in, 16)
            with sp.Fori(0, UNITS // RING) as rnd:
                for slot in range(RING):
                    load(rnd, slot)
            for slot in range(UNITS % RING):
                load(UNITS // RING, slot)
            sp_block2(sp)

        @block.gpsimd
        def _(pool):
            for l in range(DEPTH):
                for v, name, n in ((V_SC, "sc_w", 3), (V_RC, "rc_w", 4), (V_RCB, "rc_b", 1), (V_BM, "b_merge", 2),
                                   (V_RGB, "rg_b", 2), (V_A, "a_param", 1)):
                    src = t[name][l:l + 1]
                    src = src.rearrange("o g (k c) -> (o g k) c", c=P) if len(src.shape) == 3 \
                        else src.rearrange("o (k c) -> (o k) c", c=P)
                    pool.dma_start(vrows[v * KD:(v + n) * KD, l, :], src).then_inc(const_in, 16)
            pool.dma_start(crows[0:KD, :], t["c_2"].rearrange("o (k c) -> (o k) c", c=P)).then_inc(const_in, 16)
            pool.dma_start(crows[KD:2 * KD, :], t["lb_logits_2"].rearrange("o (k c) -> (o k) c", c=P)).then_inc(const_in, 16)
            pool.wait_ge(setup_dve, 1)
            pool.dma_start(mod[0:1, :], t["b_ada_2"]).then_inc(bada_in, 16)
            lg3 = t["ln_g"].rearrange("l n d -> (l n) d")
            lb3 = t["ln_b"].rearrange("l n d -> (l n) d")

            def norm_rows(n):
                pool.wait_ge(rows_free, n + 1)
                pool.dma_start(lnrow[:, 0, :], lg3[bass.ds(n, 1), :].partition_broadcast(P)).then_inc(rows_in, 16)
                pool.dma_start(lnrow[:, 1, :], lb3[bass.ds(n, 1), :].partition_broadcast(P)).then_inc(rows_in, 16)

            with pool.Fori(0, DEPTH) as l:
                norm_rows(l * 3)
                norm_rows(l * 3 + 1)
                for i in range(UNITS_MERGE):
                    if i < 2:
                        pool.wait_ge(yblo_done, l * 2 + 3)
                    else:
                        pool.wait_ge(ada_used, l * 12 + (i - 1))
                    pool.dma_start(adaraw[:, i % 2, :], t["ada"][bass.ds(l * 12 + i, 1), :, :].rearrange(
                        "o p n -> p (o n)")).then_inc(ada_in[i % 2], 16)
                norm_rows(l * 3 + 2)
            pool_block2(pool)

        @block.tensor
        def _(pe):
            def weights_ready(rnd, slot):
                pe.wait_ge(lo_done, unit_no(rnd, slot) + 1 + RING)

            def cols_unit(rnd, slot, xh, xl, outs):
                weights_ready(rnd, slot)
                for tile in range(2):
                    for k in range(KD):
                        c = k * 256 + tile * P
                        wh, wl = whi[:, slot, c:c + P], wlo[:, slot, c:c + P]
                        nc.tensor.matmul(outs[tile], wh, xh[:, k, :], start=k == 0, stop=False)
                        nc.tensor.matmul(outs[tile], wh, xl[:, k, :], start=False, stop=False)
                        last = nc.tensor.matmul(outs[tile], wl, xh[:, k, :], start=False, stop=k == KD - 1)
                last.then_inc(used, 1)

            def tokens_unit(rnd, slot, xh, xl, b):
                weights_ready(rnd, slot)
                for i in range(TT):
                    o = bank(b, i * T, (i + 1) * T)
                    for k in range(KD):
                        wh, wl = whi[:, slot, k * 256:(k + 1) * 256], wlo[:, slot, k * 256:(k + 1) * 256]
                        h, lo = xh[:, k, i * P:(i + 1) * P], xl[:, k, i * P:(i + 1) * P]
                        nc.tensor.matmul(o, h, wh, start=k == 0, stop=False)
                        nc.tensor.matmul(o, h, wl, start=False, stop=False)
                        last = nc.tensor.matmul(o, lo, wh, start=False, stop=k == KD - 1)
                last.then_inc(used, 1)

            def rows_unit(rnd, slot, hh, hl, start, stop):
                weights_ready(rnd, slot)
                for i in range(TT):
                    for k in range(2):
                        h, lo = hh[:, k, i * P:(i + 1) * P], hl[:, k, i * P:(i + 1) * P]
                        for n in range(2):
                            c = k * D + n * 512
                            o = bank(4 + 2 * i + n)
                            nc.tensor.matmul(o, h, whi[:, slot, c:c + 512], start=start and k == 0, stop=False)
                            nc.tensor.matmul(o, h, wlo[:, slot, c:c + 512], start=False, stop=False)
                        for n in range(2):
                            c = k * D + n * 512
                            last = nc.tensor.matmul(bank(4 + 2 * i + n), lo, whi[:, slot, c:c + 512],
                                                    start=False, stop=stop and k == 1)
                    if stop and i == 0:
                        last.then_inc(y0_done, 1)
                last.then_inc(used, 1)

            def transpose_x(n, src):
                for i in range(TT):
                    pe.wait_ge(x_done, n * 2 + (i + 1))
                    for b in range(2):
                        for k in range(4 * b, 4 * b + 4):
                            last = nc.tensor.transpose(xT_banks(i)[:, k, :], src[:, i, k * P:(k + 1) * P], eye[:, :])
                        last.then_inc(xT_ps, 1)

            def open_sums():
                for b in range(4, 8):
                    nc.tensor.matmul(bank(b), zero_w[:, :], xThi[:, 0:2, :].rearrange("p k t -> p (k t)"),
                                     start=True, stop=False)

            def ffn(base, f, n):
                pe.wait_ge(xTlo_done, n * 4 + 4)
                cols_unit(*at(base, 0), xThi, xTlo, [bank(0, 0, T), bank(1, 0, T)])
                cols_unit(*at(base, 1), xThi, xTlo, [bank(0, T), bank(1, T)])
                pe.wait_ge(setup_dve, 2)
                open_sums()
                with pe.Fori(0, FFN_STEPS // 2) as i:
                    for s in range(2):
                        o, par = 2 + 3 * s, 1 - s
                        cols_unit(*at(base + 2 * i, o), xThi, xTlo, [bank(2 * par, 0, T), bank(2 * par + 1, 0, T)])
                        cols_unit(*at(base + 2 * i, o + 1), xThi, xTlo, [bank(2 * par, T), bank(2 * par + 1, T)])
                        pe.wait_ge(hlo_done, f * FFN_STEPS + 2 * i + s + 1)
                        rows_unit(*at(base + 2 * i, o + 2), hhi[:, 1 - par], hlo[:, 1 - par], False, False)
                pe.wait_ge(hlo_done, (f + 1) * FFN_STEPS)
                rows_unit(*at(base, UNITS_FFN - 1), hhi[:, 0], hlo[:, 0], False, True)

            pe.wait_ge(eye_in, 16)
            transpose_x(0, x)
            pe.wait_ge(const_in, 16 * NCONST)
            for l in range(DEPTH):
                nc.tensor.transpose(bank(4 + l, 0, NVEC * KD), vrows[:, l, :], eye[0:NVEC * KD, 0:NVEC * KD])
            nc.tensor.transpose(bank(6, 0, 2 * KD), crows[:, :], eye[0:2 * KD, 0:2 * KD]).then_inc(setup_pe, 1)

            with pe.Fori(0, DEPTH) as l:
                lay = l * ROUNDS_LAYER
                ffn(lay, l * 2, l * 3)
                transpose_x(l * 3 + 1, x)
                with pe.Fori(0, 2) as hf:
                    pe.wait_ge(xTlo_done, l * 12 + 8)
                    base = lay + OFF_MIX // RING + hf * (UNITS_HALF // RING)
                    g = l * 2 + hf
                    for u, unit in enumerate(HALF):
                        rnd, slot = at(base, u)
                        if unit in PROJ_UNITS:
                            j = PROJ_UNITS.index(unit)
                            b = j % 4
                            pe.wait_ge(bank_free[b], g * BANK_USES[b] + (j // 4 + 1))
                            cols_unit(rnd, slot, xThi, xTlo, [bank(b, 0, T), bank(b, T)])
                            continue
                        pe.wait_ge(xclo_done, g * 2 + 2)
                        pe.wait_ge(gates_read, g + 1)
                        weights_ready(rnd, slot)
                        for gt in range(2):
                            for a in range(2):
                                for jt in range(2):
                                    o = halves(4, 4)[:, gt * 4 + a * 2 + jt, :]
                                    for k in range(2):
                                        c = ((gt * 2 + a) * 2 + k) * 256 + jt * P
                                        wh, wl = whi[:, slot, c:c + P], wlo[:, slot, c:c + P]
                                        nc.tensor.matmul(o, wh, xchi[:, 2 * a + k, :], start=k == 0, stop=False)
                                        nc.tensor.matmul(o, wh, xclo[:, 2 * a + k, :], start=False, stop=False)
                                        last = nc.tensor.matmul(o, wl, xchi[:, 2 * a + k, :], start=False, stop=k == 1)
                        last.then_inc(used, 1)
                base = lay + OFF_MERGE // RING
                for i, (kind, q) in enumerate(MERGE):
                    if kind == "conv":
                        pe.wait_ge(yalo_done, l * 4 + 4)
                        pe.wait_ge(bank_free[q], (l * 2 + 2) * BANK_USES[q] + 1)
                        cols_unit(*at(base, i), yahi, yalo, [bank(q, 0, T), bank(q, T)])
                    elif kind == "rnn":
                        pe.wait_ge(yblo_done, l * 2 + 3)
                        pe.wait_ge(merged, l * 8 + q + 1)
                        cols_unit(*at(base, i), ybhi, yblo, [bank(q, 0, T), bank(q, T)])
                    else:
                        pe.wait_ge(mlo_done, l * 4 + q + 1)
                        rows_unit(*at(base, i), xThi[:, 2 * q:2 * q + 2], xTlo[:, 2 * q:2 * q + 2], q == 0, q == 3)
                transpose_x(l * 3 + 2, x)
                ffn(lay + OFF_FFN2 // RING, l * 2 + 1, l * 3 + 2)
                transpose_x(l * 3 + 3, x)
            pe_block2(pe, cols_unit, tokens_unit, rows_unit, transpose_x, open_sums)

        @block.scalar
        def _(act):
            act_fn = nc.scalar.activation

            def split(rnd, slot, first=False):
                if not first:
                    act.wait_ge(used, unit_no(rnd, slot) - RING + 1)
                act.wait_ge(loaded[slot], rnd * 16 + 16)
                act_fn(whi[:, slot, :], raw[:, slot, :], ACT.Copy).then_inc(hi_done, 1)

            def turn(base, o):
                split(*at(base, o + RING))

            def split_xT(n):
                for i in range(TT):
                    for b in range(2):
                        act.wait_ge(xT_ps, n * 4 + (2 * i + b + 1))
                        ks = slice(4 * b, 4 * b + 4)
                        act_fn(xThi[:, ks, i * P:(i + 1) * P], xT_banks(i)[:, ks, :], ACT.Copy).then_inc(xThi_done, 1)

            def silu(par, base, o):
                act.wait_ge(used, unit_no(*at(base, o)) + 1)
                src = banks(2 * par, 2).rearrange("p (c u t) -> p c u t", u=2, t=T)[:, :, 0, :]
                act_fn(sil[:, :, :], src, ACT.Silu).then_inc(silu_done, 1)

            def hid_hi(par, count):
                act.wait_ge(hid_done, count)
                act_fn(hhi[:, par], hid[:, par], ACT.Copy).then_inc(hhi_done, 1)

            def norm(n):
                act_fn(spare[:, :], eps[:, 0:1], ACT.Sqrt)
                act.wait_ge(mv_done, n + 1)
                act_fn(std[:, :, 0], mv[:, :, 1], ACT.Sqrt, bias=eps[:, 0:1]).then_inc(std_done, 1)

            def ffn(base, f):
                turn(base, 0)
                silu(0, base, 1)
                hid_hi(0, f * FFN_STEPS + 1)
                turn(base, 1)
                with act.Fori(0, FFN_STEPS // 2) as i:
                    for s in range(2):
                        o, par = 2 + 3 * s, 1 - s
                        turn(base + 2 * i, o)
                        silu(par, base + 2 * i, o + 1)
                        hid_hi(par, f * FFN_STEPS + 2 * i + s + 2)
                        turn(base + 2 * i, o + 1)
                        turn(base + 2 * i, o + 2)

            split_xT(0)
            for slot in range(RING):
                split(0, slot, first=True)
            act.wait_ge(setup_dve, 3)
            act_fn(spt[:, 1, :], spt[:, 0, :], ACT.Exp, scale=-1.0).then_inc(setup_act, 1)
            act_fn(lbt[:, 3:5, :], lbt[:, 1:3, :], ACT.Exp).then_inc(setup_act, 1)
            act_fn(csil[:, :], cvec[:, 0, :], ACT.Tanh, scale=0.5).then_inc(setup_act, 1)
            with act.Fori(0, DEPTH) as l:
                lay = l * ROUNDS_LAYER
                ffn(lay, l * 2)
                norm(l * 3)
                split_xT(l * 3 + 1)
                turn(lay, UNITS_FFN - 1)
                with act.Fori(0, 2) as hf:
                    base = lay + OFF_MIX // RING + hf * (UNITS_HALF // RING)
                    g = l * 2 + hf
                    act.wait_ge(half_start, g + 1)
                    act.wait_ge(yblo_done, g + 1)
                    for u, (name, a) in enumerate(HALF):
                        turn(base, u)
                        if name == "gates":
                            for c in range(4):
                                act_fn(tt_[:, c, :], halves(4, 4)[:, 4 + c, :], ACT.Tanh, bias=now[:, V_RGB + 1, c:c + 1],
                                       scale=0.5)
                            act.drain()
                            for c in range(4):
                                ins = act_fn(tt_[:, c, :], tt_[:, c, :], ACT.Tanh, bias=now[:, V_A, c:c + 1],
                                             scale=now[:, V_A, c:c + 1])
                            ins.then_inc(t_done, 1)
                            for c in range(4):
                                ins = act_fn(gin[:, c, :], halves(4, 4)[:, c, :], ACT.Tanh, bias=now[:, V_RGB, c:c + 1],
                                             scale=0.5)
                            ins.then_inc(gates_read, 1)
                            act.wait_ge(t_read, g + 1)
                            act_fn(tt_[:, :, :], tt_[:, :, :], ACT.Sqrt).then_inc(sqrt_done, 1)
                            continue
                        hd = g * 2 + a
                        kt = bass.ds(hf * 4 + 2 * a, 2)
                        two = slice(2 * a, 2 * a + 2)
                        src, free = proj(name, a)
                        if name == "x_r":
                            act.wait_ge(xc_done, hd + 1)
                            act_fn(xrp[:, :, 3:], src, ACT.Copy).then_inc(free, 1)
                            act.drain()
                            for jt in range(2):
                                c = 2 * a + jt
                                ins = act_fn(xc[:, c, :], xrp[:, jt, 0:T], ACT.Identity,
                                             bias=now[:, V_RCB, c:c + 1], scale=now[:, V_RC, c:c + 1])
                            ins.then_inc(xc_part, 1)
                            act.wait_ge(xc_done, hd + 2)
                            act_fn(xchi[:, two, :], xc[:, two, :], ACT.Copy).then_inc(xchi_done, 1)
                        elif name == "y_r":
                            act_fn(gel[:, two, :], src, ACT.Gelu_apprx_tanh).then_inc(free, 1)
                        elif name == "c_gate":
                            act.wait_ge(cv_part, hd + 1)
                            act_fn(zpad[:, :, 2:], src, ACT.Copy).then_inc(free, 1)
                        elif name == "v" and a == 1:
                            act.wait_ge(yb_done, g + 1)
                            act_fn(ybhi[:, bass.ds(hf * 4, 4), :], gel[:, :, :], ACT.Copy).then_inc(ybhi_done, 1)
                        elif name == "b_gate":
                            act.wait_ge(cv_done, hd + 1)
                            act_fn(yahi[:, kt, :], cv[:, :, :], ACT.Copy).then_inc(yahi_done, 1)
                        elif name in ("g_a", "g_b"):
                            dst, vec = (ga, V_BM) if name == "g_a" else (gb, V_BM + 1)
                            for jt in range(2):
                                c = 2 * a + jt
                                ins = act_fn(dst[:, bass.ds(hf * 4 + c, 1), :].rearrange("p o t -> p (o t)"),
                                             src[:, jt, :], ACT.Tanh, bias=now[:, vec, c:c + 1], scale=0.5)
                            ins.then_inc(free, 1)
                base = lay + OFF_MERGE // RING
                for i, (kind, q) in enumerate(MERGE):
                    if i < UNITS_MERGE - 1:
                        turn(base, i)
                    if kind == "rnn":
                        act.wait_ge(m_done, l * 4 + q + 1)
                        act_fn(xThi[:, 2 * q:2 * q + 2, :], ga[:, 2 * q:2 * q + 2, :], ACT.Copy, scale=0.5).then_inc(mhi_done, 1)
                norm(l * 3 + 1)
                split_xT(l * 3 + 2)
                turn(base, UNITS_MERGE - 1)
                ffn(lay + OFF_FFN2 // RING, l * 2 + 1)
                norm(l * 3 + 2)
                split_xT(l * 3 + 3)
                turn(lay + OFF_FFN2 // RING, UNITS_FFN - 1)
            act_block2(act, turn, split_xT, silu, hid_hi)

        @block.vector
        def _(dve):
            v = nc.vector

            def refine(r, root, var, t):
                v.reciprocal(r, root)
                dve.drain()
                v.tensor_tensor(t, r, r, ALU.mult)
                dve.drain()
                v.tensor_tensor(t, t, var, ALU.mult)
                dve.drain()
                v.tensor_scalar(t, t, -0.5, 1.5, ALU.mult, ALU.add)
                dve.drain()
                v.tensor_tensor(r, r, t, ALU.mult)
                dve.drain()

            def split(rnd, slot):
                dve.wait_ge(hi_done, unit_no(rnd, slot) + 1)
                v.tensor_tensor(wlo[:, slot, :], raw[:, slot, :], whi[:, slot, :].bitcast(F32),
                                ALU.subtract).then_inc(lo_done, 1)

            def turn(base, o):
                split(*at(base, o + RING))

            def split_xT(n):
                for i in range(TT):
                    for b in range(2):
                        dve.wait_ge(xThi_done, n * 4 + (2 * i + b + 1))
                        ks, sl = slice(4 * b, 4 * b + 4), slice(i * P, (i + 1) * P)
                        v.tensor_tensor(xTlo[:, ks, sl], xT_banks(i)[:, ks, :], xThi[:, ks, sl].bitcast(F32),
                                        ALU.subtract).then_inc(xTlo_done, 1)

            def hidden(par, count):
                dve.wait_ge(silu_done, count)
                up = banks(2 * par, 2).rearrange("p (c u t) -> p c u t", u=2, t=T)[:, :, 1, :]
                v.scalar_tensor_tensor(hid[:, par], sil[:, :, :], 0.5, up, ALU.mult, ALU.mult).then_inc(hid_done, 1)

            def hid_lo(par, count):
                dve.wait_ge(hhi_done, count)
                v.tensor_tensor(hlo[:, par], hid[:, par], hhi[:, par].bitcast(F32), ALU.subtract).then_inc(hlo_done, 1)

            def norm(n, units):
                for i in range(TT):
                    if i == 0:
                        dve.wait_ge(y0_done, n + 1)
                    else:
                        dve.wait_ge(used, units)
                    v.scalar_tensor_tensor(x[:, i, :], x[:, i, :], ALPHA, banks(4 + 2 * i, 2), ALU.mult, ALU.add)
                    dve.drain()
                    for n2 in range(2):
                        v.bn_stats(stats[:, i, n2, :], x[:, i, n2 * 512:(n2 + 1) * 512])
                    dve.drain()
                    ins = v.bn_aggr(mv[:, i, :], stats[:, i, :, :].rearrange("p a b -> p (a b)"))
                ins.then_inc(mv_done, 1)
                dve.drain()
                dve.wait_ge(rows_in, n * 32 + 32)
                v.tensor_scalar(var[:, :, 0], mv[:, :, 1], LN_EPS, None, ALU.add)
                for i in range(TT):
                    v.scalar_tensor_tensor(x[:, i, :], x[:, i, :], mv[:, i, 0:1], lnrow[:, 0, :], ALU.subtract, ALU.mult)
                    if i == 0:
                        dve.drain()
                        dve.wait_ge(std_done, n + 1)
                        refine(rstd[:, :, 0], std[:, :, 0], var[:, :, 0], newt[:, 0:TT])
                    else:
                        dve.drain()
                    v.scalar_tensor_tensor(x[:, i, :], x[:, i, :], rstd[:, i, 0:1], lnrow[:, 1, :], ALU.mult,
                                           ALU.add).then_inc(x_done, 1)
                dve.drain()
                v.memset(tick[:, :], 0.0).then_inc(rows_free, 1)

            def ffn(base, f):
                turn(base, 0)
                hidden(0, f * FFN_STEPS + 1)
                hid_lo(0, f * FFN_STEPS + 1)
                turn(base, 1)
                with dve.Fori(0, FFN_STEPS // 2) as i:
                    for s in range(2):
                        o, par = 2 + 3 * s, 1 - s
                        turn(base + 2 * i, o)
                        hidden(par, f * FFN_STEPS + 2 * i + s + 2)
                        hid_lo(par, f * FFN_STEPS + 2 * i + s + 2)
                        turn(base + 2 * i, o + 1)
                        turn(base + 2 * i, o + 2)

            v.memset(zero_w[:, :].bitcast(F32), 0.0)
            v.memset(ones[:, :], 1.0)
            v.memset(eps[:, 0:1], LN_EPS)
            v.memset(eps[:, 1:2], RMS_EPS)
            v.memset(mod[:, :], 0.0).then_inc(setup_dve, 1)
            dve.sem_inc(lo_done, RING)
            for free in (*bank_free, gates_read, rows_free, yblo_done, xc_done, cv_part):
                dve.sem_inc(free, 1)
            dve.wait_ge(x_in, 16)
            dve.sem_inc(x_done, 2)
            split_xT(0)
            for slot in range(RING):
                split(0, slot)
            dve.wait_ge(setup_pe, 1)
            for l in range(DEPTH):
                v.tensor_copy(vecs[:, l].rearrange("p v h k -> p (v h k)"), bank(4 + l, 0, NVEC * KD))
            v.tensor_copy(cvec[:, :, :].rearrange("p a k -> p (a k)"), bank(6, 0, 2 * KD))
            dve.drain()
            v.memset(tick[:, :], 0.0).then_inc(setup_dve, 1)
            for l in range(DEPTH):
                half = vecs[:, l, V_BM:V_A].rearrange("p v h k -> p (v h k)")
                v.tensor_scalar(half, half, 0.5, None, ALU.mult)
                v.tensor_copy(spt[:, 4, l * KD:(l + 1) * KD], vecs[:, l, V_A].rearrange("p h k -> p (h k)"))
            v.tensor_tensor(lbt[:, 0, :], cvec[:, 1, 0:4], cvec[:, 1, 4:8], ALU.max)
            dve.drain()
            v.tensor_scalar(spt[:, 0, :], spt[:, 4, :], -1.0, None, ALU.mult)
            v.tensor_tensor(lbt[:, 1, :], cvec[:, 1, 0:4], lbt[:, 0, :], ALU.subtract)
            v.tensor_tensor(lbt[:, 2, :], cvec[:, 1, 4:8], lbt[:, 0, :], ALU.subtract)
            dve.drain()
            v.tensor_tensor(spt[:, 0, :], spt[:, 4, :], spt[:, 0, :], ALU.max).then_inc(setup_dve, 1)
            dve.wait_ge(setup_act, 2)
            v.tensor_scalar(spt[:, 2, :], spt[:, 1, :], 2.0, None, ALU.add)
            dve.drain()
            v.reciprocal(spt[:, 2, :], spt[:, 2, :])
            dve.drain()
            v.tensor_tensor(spt[:, 1, :], spt[:, 1, :], spt[:, 2, :], ALU.mult)
            dve.drain()
            v.tensor_tensor(spt[:, 2, :], spt[:, 1, :], spt[:, 1, :], ALU.mult)
            v.memset(spt[:, 3, :], 1.0 / 17)
            dve.drain()
            for odd in (15, 13, 11, 9, 7, 5, 3, 1):
                v.tensor_tensor(spt[:, 3, :], spt[:, 3, :], spt[:, 2, :], ALU.mult)
                dve.drain()
                v.tensor_scalar(spt[:, 3, :], spt[:, 3, :], 1.0 / odd, None, ALU.add)
                dve.drain()
            v.tensor_tensor(spt[:, 3, :], spt[:, 3, :], spt[:, 1, :], ALU.mult)
            v.tensor_scalar(spt[:, 4, :], spt[:, 4, :], -1.0, 0.0, ALU.mult, ALU.max)
            dve.drain()
            v.tensor_scalar(spt[:, 4, :], spt[:, 4, :], 2.0, None, ALU.mult)
            v.tensor_tensor(lbt[:, 5, :], lbt[:, 3, :], lbt[:, 4, :], ALU.add)
            dve.drain()
            v.reciprocal(lbt[:, 5, :], lbt[:, 5, :])
            for l in range(DEPTH):
                v.scalar_tensor_tensor(vecs[:, l, V_A].rearrange("p h k -> p (h k)"), spt[:, 3, l * KD:(l + 1) * KD],
                                       4.0, spt[:, 4, l * KD:(l + 1) * KD], ALU.mult, ALU.add)
            dve.drain()
            v.tensor_tensor(lbt[:, 0, :], lbt[:, 3, :], lbt[:, 5, :], ALU.mult)
            dve.drain()
            v.tensor_scalar(lbt[:, 1, :], lbt[:, 0, :], -0.5, 0.5, ALU.mult, ALU.add)
            v.tensor_scalar(lbt[:, 2, :], lbt[:, 0, :], 0.5, 0.5, ALU.mult, ALU.add)
            dve.wait_ge(setup_act, 3)
            v.scalar_tensor_tensor(csil[:, :], csil[:, :], 1.0, cvec[:, 0, :], ALU.add, ALU.mult)
            dve.drain()
            v.tensor_scalar(csil[:, :], csil[:, :], 0.5, None, ALU.mult)
            dve.drain()
            dve.wait_ge(bada_in, 16)
            with dve.Fori(0, DEPTH) as l:
                lay = l * ROUNDS_LAYER
                ffn(lay, l * 2)
                norm(l * 3, unit_no(*at(lay, UNITS_FFN)))
                split_xT(l * 3 + 1)
                turn(lay, UNITS_FFN - 1)
                with dve.Fori(0, 2) as hf:
                    base = lay + OFF_MIX // RING + hf * (UNITS_HALF // RING)
                    g = l * 2 + hf
                    last_bank = (len(PROJ_UNITS) - 1) % 4
                    dve.wait_ge(bank_free[last_bank], g * BANK_USES[last_bank] + 1)
                    v.memset(zpad[:, :, 0:2], 0.0)
                    v.memset(xrp[:, :, 0:3], 0.0)
                    v.tensor_copy(now[:, :, :], vecs[:, bass.ds(l, 1), :, bass.ds(hf, 1), :].rearrange(
                        "p o v h k -> p (o v h) k")).then_inc(half_start, 1)
                    for u, (name, a) in enumerate(HALF):
                        turn(base, u)
                        if name == "gates":
                            dve.wait_ge(t_done, g + 1)
                            v.tensor_scalar(rr[:, :, :], tt_[:, :, :], 1.0, None, ALU.add).then_inc(t_read, 1)
                            dve.drain()
                            v.reciprocal(rr[:, 0:2, :], rr[:, 0:2, :])
                            continue
                        hd = g * 2 + a
                        kt = bass.ds(hf * 4 + 2 * a, 2)
                        two = slice(2 * a, 2 * a + 2)
                        src, free = proj(name, a)
                        if name == "x_r":
                            dve.wait_ge(xc_part, hd + 1)
                            for tap in range(1, 4):
                                for jt in range(2):
                                    c = 2 * a + jt
                                    ins = v.scalar_tensor_tensor(xc[:, c, :], xrp[:, jt, tap:tap + T],
                                                                 now[:, V_RC + tap, c:c + 1], xc[:, c, :], ALU.mult,
                                                                 ALU.add)
                                if tap < 3:
                                    dve.drain()
                            ins.then_inc(xc_done, 1)
                            dve.wait_ge(xchi_done, hd + 1)
                            v.tensor_tensor(xclo[:, two, :], xc[:, two, :], xchi[:, two, :].bitcast(F32),
                                            ALU.subtract).then_inc(xclo_done, 1)
                        elif name == "v":
                            _, c_free = proj("c_gate", a)
                            dve.wait_ge(c_free, g * BANK_USES[proj_bank("c_gate", a)] + (
                                PROJ_UNITS.index(("c_gate", a)) // 4 + 2))
                            v.tensor_tensor(zpad[:, :, 2:], zpad[:, :, 2:], src, ALU.mult).then_inc(free, 1)
                            dve.drain()
                            for tap in range(3):
                                for jt in range(2):
                                    c = 2 * a + jt
                                    w = now[:, V_SC + tap, c:c + 1]
                                    if tap == 0:
                                        v.tensor_scalar(cv[:, jt, :], zpad[:, jt, 0:T], w, None, ALU.mult)
                                    else:
                                        ins = v.scalar_tensor_tensor(cv[:, jt, :], zpad[:, jt, tap:tap + T], w,
                                                                     cv[:, jt, :], ALU.mult, ALU.add)
                                if tap < 2:
                                    dve.drain()
                            ins.then_inc(cv_part, 1)
                        elif name == "b_gate":
                            dve.drain()
                            v.tensor_tensor(cv[:, :, :], cv[:, :, :], src, ALU.mult).then_inc(free, 1)
                            dve.drain()
                            v.memset(tick[:, :], 0.0).then_inc(cv_done, 1)
                            dve.wait_ge(yahi_done, hd + 1)
                            v.tensor_tensor(yalo[:, kt, :], cv[:, :, :], yahi[:, kt, :].bitcast(F32),
                                            ALU.subtract).then_inc(yalo_done, 1)
                        if (name, a) == ("c_gate", 0):
                            v.reciprocal(rr[:, 2:4, :], rr[:, 2:4, :])
                            dve.wait_ge(gates_read, g + 2)
                            v.scalar_tensor_tensor(gin[:, :, :], gin[:, :, :], 1.0, xc[:, :, :], ALU.add, ALU.mult)
                            dve.drain()
                        elif (name, a) == ("b_gate", 0):
                            dve.wait_ge(sqrt_done, g + 1)
                            v.tensor_tensor(tt_[:, :, :], tt_[:, :, :], rr[:, :, :], ALU.mult)
                            dve.drain()
                            v.memset(tt_[:, :, 0:1], 0.5)
                            dve.drain()
                        elif (name, a) == ("g_a", 0):
                            v.tensor_scalar(rr[:, :, :], rr[:, :, :], 2.0, -1.0, ALU.mult, ALU.add)
                            v.tensor_tensor(gin[:, :, :], gin[:, :, :], tt_[:, :, :], ALU.mult)
                            dve.drain()
                        elif (name, a) == ("g_b", 0):
                            for c in range(4):
                                v.tensor_tensor_scan(tt_[:, c, :], rr[:, c, :], gin[:, c, :], 0.0, ALU.mult, ALU.add)
                            dve.drain()
                            v.tensor_tensor(gel[:, :, :], gel[:, :, :], tt_[:, :, :], ALU.mult).then_inc(yb_done, 1)
                        elif (name, a) == ("v", 1):
                            dve.wait_ge(ybhi_done, g + 1)
                            v.tensor_tensor(yblo[:, bass.ds(hf * 4, 4), :], gel[:, :, :],
                                            ybhi[:, bass.ds(hf * 4, 4), :].bitcast(F32),
                                            ALU.subtract).then_inc(yblo_done, 1)
                base = lay + OFF_MERGE // RING
                for i, (kind, q) in enumerate(MERGE):
                    if i < UNITS_MERGE - 1:
                        turn(base, i)
                    two = slice(2 * q, 2 * q + 2)
                    if kind == "conv":
                        v.scalar_tensor_tensor(ga[:, two, :], ga[:, two, :], 1.0, halves(q), ALU.add,
                                               ALU.mult).then_inc(merged, 1)
                    elif kind == "rnn":
                        v.scalar_tensor_tensor(gb[:, two, :], gb[:, two, :], 1.0, halves(q), ALU.add,
                                               ALU.mult).then_inc(merged, 1)
                        dve.drain()
                        v.tensor_tensor(ga[:, two, :], ga[:, two, :], gb[:, two, :], ALU.add).then_inc(m_done, 1)
                        dve.wait_ge(mhi_done, l * 4 + q + 1)
                        v.scalar_tensor_tensor(xTlo[:, two, :], ga[:, two, :], 0.5, xThi[:, two, :].bitcast(F32),
                                               ALU.mult, ALU.subtract).then_inc(mlo_done, 1)
                    dve.drain()
                    dve.wait_ge(ada_in[i % 2], l * 96 + 16 * (i // 2) + 16)
                    k = 2 * (i // 3)
                    if i % 3 < 2:
                        part = mod[:, bass.ds(l * 3072, 2048)]
                        ins = v.scalar_tensor_tensor(part, adaraw[:, i % 2, :], csil[:, k + i % 3:k + i % 3 + 1], part,
                                                     ALU.mult, ALU.add)
                    else:
                        part = mod[:, bass.ds(l * 3072 + 2048, 1024)]
                        v.scalar_tensor_tensor(part, adaraw[:, i % 2, 0:D], csil[:, k:k + 1], part, ALU.mult, ALU.add)
                        dve.drain()
                        ins = v.scalar_tensor_tensor(part, adaraw[:, i % 2, D:], csil[:, k + 1:k + 2], part,
                                                     ALU.mult, ALU.add)
                    ins.then_inc(ada_used, 1)
                norm(l * 3 + 1, unit_no(*at(base, UNITS_MERGE)))
                split_xT(l * 3 + 2)
                turn(base, UNITS_MERGE - 1)
                ffn(lay + OFF_FFN2 // RING, l * 2 + 1)
                norm(l * 3 + 2, unit_no(*at(lay, UNITS_LAYER)))
                split_xT(l * 3 + 3)
                turn(lay + OFF_FFN2 // RING, UNITS_FFN - 1)
            dve_block2(dve, turn, split_xT, hid_lo, refine)


_INS = ["x", "w_in", "b_merge", "sc_w", "rc_w", "rc_b", "rg_w", "rg_b", "a_param", "w_out_conv", "w_out_rnn", "w_o",
        "ffn_w1", "ffn_w2", "ln_g", "ln_b", "c_2", "w_ada_2", "b_ada_2", "norm1_g_2", "norm2_g_2", "w_in_2",
        "lb_logits_2", "rec_out_g_2", "q_norm_g_2", "k_norm_g_2", "idx_k_norm_g_2", "idx_k_norm_b_2",
        "attn_out_g_2", "rel_bias_2", "w_out_2", "w_rg_2", "b_rg_2", "w_re_2", "b_re_2", "w1_2", "w3_2", "w2_2"]

STREAMED = ["w_in", "rg_w", "w_out_conv", "w_out_rnn", "w_o", "ffn_w1", "ffn_w2", "w_ada_2", "w_out_2", "w1_2", "w3_2",
            "w2_2"]


def kernel(**inputs):
    import concourse.bacc as _bacc
    from concourse.bass_utils import run_bass_kernel_spmd as _run

    nc = _bacc.Bacc("TRN2", target_bir_lowering=False, num_devices=1)
    arrays = {name: np.ascontiguousarray(inputs[name]) for name in _INS}
    arrays["stream"], arrays["ada"] = weight_stream(arrays)
    for name in STREAMED:
        del arrays[name]
    arrays.update(constants())
    t = {name: nc.dram_tensor(name, a.shape, mybir.dt.from_np(a.dtype), kind="ExternalInput").ap()
         for name, a in arrays.items()}
    t["scratch"] = nc.dram_tensor("scratch", [A_HEADS, HANK], F32).ap()
    out = nc.dram_tensor("out", [1, T, D], F32, kind="ExternalOutput").ap()
    build(nc, t, out)
    r = _run(nc, [arrays], core_ids=[0])
    return r.results[0]["out"]
```

```python
from contextlib import ExitStack

import numpy as np

import concourse.bass as bass
from concourse import mybir

F32 = mybir.dt.float32
F32R = mybir.dt.float32r
U8 = mybir.dt.uint8
ALU = mybir.AluOpType
ACT = mybir.ActivationFunctionType
AX_X = mybir.AxisListType.X
AX_XY = mybir.AxisListType.XY

P = 128
T = 256
TT = T // P
D = 1024
KD = D // P
DEPTH = 2
D_FF = 2816
FFN_STEPS = D_FF // 256
HEADS = 4
LN_EPS = 1e-5
RMS_EPS = 1e-6
ALPHA = (2.0 * DEPTH) ** 0.25
RING = 3
UNIT = 2048
UNITS_FFN = 3 * FFN_STEPS
UNITS_HALF = 15
UNITS_MERGE = 12
OFF_MIX = UNITS_FFN
OFF_MERGE = OFF_MIX + 2 * UNITS_HALF
OFF_FFN2 = OFF_MERGE + UNITS_MERGE
UNITS_LAYER = OFF_FFN2 + UNITS_FFN
assert UNITS_LAYER % RING == 0 and UNITS_HALF % RING == 0
ROUNDS_LAYER = UNITS_LAYER // RING
ROUND_2 = DEPTH * ROUNDS_LAYER
EXPERTS = 16
MOE_STEPS = 2 * EXPERTS
OFF_WOUT2 = 16
OFF_MOE = 20
UNITS = DEPTH * UNITS_LAYER + OFF_MOE + 3 * MOE_STEPS
V_SC, V_RC, V_RCB, V_BM, V_RGB, V_A, NVEC = 0, 3, 7, 8, 10, 12, 13
PROJ = {"x_r": 3 * D, "y_r": 4 * D, "c_gate": D, "v": 2 * D, "b_gate": 0, "g_a": 5 * D, "g_b": 6 * D}
HALF = [("x_r", 0), ("x_r", 1), ("y_r", 0), ("y_r", 1), ("gates", None)] + [
    (name, a) for a in range(2) for name in ("c_gate", "v", "b_gate", "g_a", "g_b")]
PROJ_UNITS = [u for u in HALF if u[0] != "gates"]
BANK_USES = [len(PROJ_UNITS[b::4]) for b in range(4)]
MERGE = [(kind, q) for kind in ("conv", "rnn", "wo") for q in range(4)]
ADA_PIECES = 12
NCONST = 6 * DEPTH + 2
IN2_COLS = [0, 256, 512, 768, 1536, 1792, 1024, 1280, 2048, 2304, 2560, 2816, 3072, 3328, 3584, 3840]
BLOCK2_LOADS = 9
TOPK = 64
BIG = 3.0e38
TAKEN = 3.3e38
A_HEADS = 8
A_DH = 64
LEVELS = 8
HANK = 384


def constants():
    rel = np.arange(HANK) - 255
    far = np.maximum(np.abs(rel), 1).astype(np.float32)
    large = 8 + (np.log(far / np.float32(8)) / np.float32(np.log(16)) * np.float32(8)).astype(np.int32)
    bucket = np.where(rel > 0, 16, 0) + np.where(np.abs(rel) < 8, np.abs(rel), np.minimum(large, 15))
    onehot = (bucket[None, :] == np.arange(32)[:, None]).astype(np.float32)
    s, t = np.arange(P)[:, None], np.arange(P)[None, :]
    masks = [s == t] + [(s // (2 * h) == t // (2 * h)) & (s % (2 * h) < h) & (t % (2 * h) >= h)
                        for h in (1, 2, 4, 8, 16, 32, 64)]
    levels = np.stack(masks, 1).astype(np.float32)
    eye = np.eye(P, dtype=np.float32)
    return {"c_onehot": onehot, "c_levels": levels, "c_eye": eye, "c_flip": np.ascontiguousarray(eye[::-1])}


def cols(w, col):
    return w[:, col:col + 256].reshape(KD, P, 256).transpose(1, 0, 2).reshape(P, UNIT)


def rows(w, row):
    return w[row:row + 256].reshape(2, P, D).transpose(1, 0, 2).reshape(P, UNIT)


def swiglu_units(steps):
    steps = list(steps)
    order = list(steps[0][:2])
    for before, (g, u, _) in zip(steps, steps[1:]):
        order += [g, u, before[2]]
    return order + [steps[-1][2]]


def weight_stream(a):
    units = []

    def ffn(l, f):
        w1, w2 = a["ffn_w1"][l, f], a["ffn_w2"][l, f]
        return swiglu_units((cols(w1, c), cols(w1, D_FF + c), rows(w2, c)) for c in range(0, D_FF, 256))

    for l in range(DEPTH):
        units += ffn(l, 0)
        for hf in range(2):
            rg = a["rg_w"][l][:, 2 * hf:2 * hf + 2].reshape(2, 2, 2, P, 256)
            units += [rg.transpose(3, 0, 1, 2, 4).reshape(P, UNIT) if name == "gates"
                      else cols(a["w_in"][l], PROJ[name] + 256 * (2 * hf + head)) for name, head in HALF]
        w = {"conv": a["w_out_conv"][l], "rnn": a["w_out_rnn"][l]}
        units += [rows(a["w_o"][l], 256 * q) if kind == "wo" else cols(w[kind], 256 * q) for kind, q in MERGE]
        units += ffn(l, 1)
    units += [cols(a["w_in_2"][0], c) for c in IN2_COLS]
    units += [rows(a["w_out_2"][0], 256 * q) for q in range(4)]
    w1, w3, w2 = a["w1_2"][0], a["w3_2"][0], a["w2_2"][0]
    units += swiglu_units((cols(w1[e], c), cols(w3[e], c), rows(w2[e], c)) for e in range(EXPERTS) for c in (0, 256))
    assert len(units) == UNITS
    ada = a["w_ada_2"][0].reshape(DEPTH, KD // DEPTH, P, ADA_PIECES, 512).transpose(0, 3, 2, 1, 4)
    return np.stack(units), ada.reshape(DEPTH * ADA_PIECES, P, UNIT)


def at(base_round, offset):
    return base_round + offset // RING, offset % RING


def build(nc, t, out):
    ctx = ExitStack()
    with ctx:
        def sb(name, shape, dt=F32, scope=ctx):
            return scope.enter_context(nc.sbuf_tensor(name, shape, dt))

        def sem(name):
            return ctx.enter_context(nc.semaphore(name))

        raw = sb("raw", [P, RING, UNIT])
        whi = sb("whi", [P, RING, UNIT], F32R)
        wlo = sb("wlo", [P, RING, UNIT], F32R)
        x = sb("x_sb", [P, TT, D])
        xThi = sb("xThi", [P, KD, T], F32R)
        xTlo = sb("xTlo", [P, KD, T], F32R)
        lnrow = sb("lnrow", [P, 2, D])
        mod = sb("mod", [P, 6 * D])
        eye = sb("eye", [P, P])
        zero_w = sb("zero_w", [P, P], F32R)
        ones = sb("ones", [P, P])
        vrows = sb("vrows", [NVEC * KD, DEPTH, P])
        crows = sb("crows", [2 * KD, P])
        tick = sb("tick", [P, 1])
        spare = sb("spare", [P, 1])
        stats = sb("stats", [P, TT, 2, 6])
        mv = sb("mv", [P, TT, 2])
        std = sb("std", [P, TT, 1])
        rstd = sb("rstd", [P, TT, 1])
        var = sb("var", [P, TT, 1])
        newt = sb("newt", [P, 32])
        eps = sb("eps", [P, 2])
        vecs = sb("vecs", [P, DEPTH, NVEC, 2, 4])
        now = sb("now", [P, NVEC, 4])
        spt = sb("spt", [P, 5, DEPTH * KD])
        cvec = sb("cvec", [P, 2, KD])
        csil = sb("csil", [P, KD])
        csil_now = sb("csil_now", [P, KD // DEPTH])
        lbt = sb("lbt", [P, 6, HEADS])
        ps = ctx.enter_context(nc.psum_tensor("ps", [P, 8 * 512], F32))

        def bank(b, a=0, e=512):
            return ps[:, b * 512 + a:b * 512 + e]

        def banks(b, n):
            return ps[:, b * 512:(b + n) * 512]

        def halves(b, n=1):
            return banks(b, n).rearrange("p (c t) -> p c t", t=T)

        def xT_banks(i):
            return banks(2 * i, 2).rearrange("p (k t) -> p k t", t=P)

        ffn_scope = ExitStack()
        sil = sb("sil", [P, 2, T], F32, ffn_scope)
        hid = sb("hid", [P, 2, 2, T], F32, ffn_scope)
        hhi = sb("hhi", [P, 2, 2, T], F32R, ffn_scope)
        hlo = sb("hlo", [P, 2, 2, T], F32R, ffn_scope)
        moe_scope = ExitStack()
        cmb = sb("cmb", [P, EXPERTS, T], F32, moe_scope)
        moe_scope.close()
        ffn_scope.close()

        mix_scope = ExitStack()
        zpad = sb("zpad", [P, 2, 2 + T], F32, mix_scope)
        xrp = sb("xrp", [P, 2, 3 + T], F32, mix_scope)
        cv = sb("cv", [P, 2, T], F32, mix_scope)
        gin = sb("gin", [P, 4, T], F32, mix_scope)
        ga = sb("ga", [P, KD, T], F32, mix_scope)
        gb = sb("gb", [P, KD, T], F32, mix_scope)
        yahi = sb("yahi", [P, KD, T], F32R, mix_scope)
        yalo = sb("yalo", [P, KD, T], F32R, mix_scope)
        ybhi = sb("ybhi", [P, KD, T], F32R, mix_scope)
        yblo = sb("yblo", [P, KD, T], F32R, mix_scope)
        head_scope = ExitStack()
        xc = sb("xc", [P, 4, T], F32, head_scope)
        gel = sb("gel", [P, 4, T], F32, head_scope)
        split_scope = ExitStack()
        xchi = sb("xchi", [P, 4, T], F32R, split_scope)
        xclo = sb("xclo", [P, 4, T], F32R, split_scope)
        split_scope.close()
        gate_scope = ExitStack()
        tt_ = sb("tt_", [P, 4, T], F32, gate_scope)
        rr = sb("rr", [P, 4, T], F32, gate_scope)
        gate_scope.close()
        head_scope.close()
        adaraw = sb("adaraw", [P, 2, UNIT], F32, mix_scope)
        mix_scope.close()

        b2 = ExitStack()
        vtok = sb("vtok", [P, TT, 512], F32, b2)
        gate = sb("gate", [P, TT, 512], F32, b2)
        qk = sb("qk", [P, TT, 1024], F32, b2)
        av = sb("av", [P, TT, 512], F32, b2)
        iqT = sb("iqT", [P, 4, T], F32, b2)
        ikT = sb("ikT", [P, T], F32, b2)
        ikd = sb("ikd", [P, TT, P], F32, b2)
        cat = sb("cat", [P, TT, D], F32, b2)
        outg = sb("outg", [P, 1024], F32, b2)
        qkg = sb("qkg", [P, 4, A_DH], F32, b2)
        small = sb("small", [P, KD, 72], F32, b2)
        iw = sb("iw", [P, TT, 8], F32, b2)
        nrm = sb("nrm", [P, 4, 32], F32, b2)
        soft = sb("soft", [P, 3, 2 * A_HEADS], F32, b2)
        top8 = sb("top8", [P, 8], F32, b2)
        flip = sb("flip", [P, P], F32, b2)
        rec_scope = ExitStack()
        levels = sb("levels", [P, LEVELS, P], U8, rec_scope)
        qT = sb("qT", [P, HEADS, T], F32, rec_scope)
        fT = sb("fT", [P, HEADS, T], F32, rec_scope)
        kT = sb("kT", [P, HEADS, T], F32, rec_scope)
        suf = sb("suf", [P, HEADS, T], F32, rec_scope)
        qdT = sb("qdT", [P, HEADS, T], F32, rec_scope)
        kdT = sb("kdT", [P, HEADS, T], F32, rec_scope)
        amat = sb("amat", [P, 2 * HEADS, P], F32, rec_scope)
        across = sb("across", [P, HEADS, P], F32, rec_scope)
        rec_scope.close()
        att_scope = ExitStack()
        score = sb("score", [P, 2, T], F32, att_scope)
        hank = sb("hank", [P, A_HEADS, T], F32, att_scope)
        qkT = sb("qkT", [P, 8, T], F32, att_scope)
        lg = sb("lg", [P, A_HEADS, T], F32, att_scope)
        pT = qk[:, :, :].rearrange("p k (h t) -> p k h t", h=A_HEADS)
        att_scope.close()
        b2.close()
        route = ExitStack()
        sb("below_router", [P, 9216], F32, route)
        rw = sb("rw", [P, KD, 20], F32, route)
        rwhi = sb("rwhi", [P, KD, 20], F32R, route)
        rwlo = sb("rwlo", [P, KD, 20], F32R, route)
        rlogT = sb("rlogT", [20, T], F32, route)
        rbias = sb("rbias", [P, 20], F32, route)
        rlog = sb("rlog", [P, TT, 20], F32, route)
        rt = sb("rt", [P, TT, 64], F32, route)
        comb = sb("comb", [P, TT, EXPERTS], F32, route)
        route.close()
        squares = lnrow[:, 1, :].rearrange("p (b c) -> p b c", b=2)
        table = lnrow[0:32, 1, 512:512 + HANK + A_HEADS]
        relv = lnrow[0:A_HEADS, 1, 512:512 + HANK]

        loaded = [sem(f"loaded{s}") for s in range(RING)]
        hi_done = sem("hi_done")
        lo_done = sem("lo_done")
        used = sem("used")
        const_in = sem("const_in")
        bada_in = sem("bada_in")
        rows_in = sem("rows_in")
        rows_free = sem("rows_free")
        setup_dve = sem("setup_dve")
        setup_act = sem("setup_act")
        setup_pe = sem("setup_pe")
        x_in = sem("x_in")
        eye_in = sem("eye_in")
        y0_done = sem("y0_done")
        silu_done = sem("silu_done")
        hid_done = sem("hid_done")
        hhi_done = sem("hhi_done")
        hlo_done = sem("hlo_done")
        mv_done = sem("mv_done")
        std_done = sem("std_done")
        x_done = sem("x_done")
        xT_ps = sem("xT_ps")
        xThi_done = sem("xThi_done")
        xTlo_done = sem("xTlo_done")
        half_start = sem("half_start")
        bank_free = [sem(f"bank_free{b}") for b in range(4)]
        xc_part = sem("xc_part")
        xc_done = sem("xc_done")
        xchi_done = sem("xchi_done")
        xclo_done = sem("xclo_done")
        cv_part = sem("cv_part")
        cv_done = sem("cv_done")
        yahi_done = sem("yahi_done")
        yalo_done = sem("yalo_done")
        gates_read = sem("gates_read")
        t_done = sem("t_done")
        t_read = sem("t_read")
        sqrt_done = sem("sqrt_done")
        yb_done = sem("yb_done")
        ybhi_done = sem("ybhi_done")
        yblo_done = sem("yblo_done")
        merged = sem("merged")
        m_done = sem("m_done")
        mhi_done = sem("mhi_done")
        mlo_done = sem("mlo_done")
        ada_in = [sem("ada_in0"), sem("ada_in1")]
        ada_used = sem("ada_used")
        ev = {name: sem(name) for name in (
            "mod0_ps mod1_ps mod2_ps mod0 mod1 mod2 "
            "gain1_in block2_in gain2_in table_in hank_in router_in rel_out "
            "ss1 std1 ss2 std2 h1_free "
            "cat_rec evac lvl_ready lvl_ps rec_in recv_ps rec_sq rec_ss rec_std "
            "ik_ps ik_mv ik_std ik_norm ikT_ps ikT qk_ss qk_std qk_norm qkT_ps qkT "
            "rel_ps rel sc0_ps sc1_ps relu0 relu1 lg0_ps lg1_ps lg0 lg1 exp0 exp1 lg_ps0 lg_ps1 "
            "pT0 pT1 av0_ps av1_ps araw att_sq att_ss att_std "
            "rw_hi rw_split routeT_ps routeT route_ps rexp_in rexp rexp2_in rexp2 comb comb_ps comb_a comb_b comb_c final").split()}
        out_done = sem("out_done")

        BASE = ROUND_2
        N_H1, N_CAT, N_H2 = 3 * DEPTH + 1, 3 * DEPTH + 2, 3 * DEPTH + 3
        EVAC_HOLD = 4
        hilo = [xTlo[:, :, :].bitcast(F32), xThi[:, :, :].bitcast(F32)]
        SPAN = [P, T]

        def by_half(m, h):
            return m[:, :, :].rearrange("p a t -> p (a t)").rearrange("p (b two s) -> p b two s", two=2, s=h)

        def row(m, n):
            return m[:, n * D:(n + 1) * D]

        AV_BANK = [6, 0]

        def pos(h):
            return h % 2 * 4 + h // 2

        def spans(i):
            return banks(4 - 4 * i, 2 + 2 * i).rearrange("p (h s) -> p h s", s=SPAN[i])

        def prob_banks(i):
            return banks(6 - 2 * i, 2 + 2 * i)

        def logits(i):
            return lnrow[:, 1, :].rearrange("p (h s) -> p h s", s=P) if i == 0 else lg[:, :, :]

        def sp_block2(sp):
            for i in range(TT):
                for half in range(2):
                    cs = slice(512 * half, 512 * half + 512)
                    sp.wait_ge(ev["final"], 2 * i + half + 1)
                    sp.dma_start(out[0, i * P:(i + 1) * P, cs], x[:, i, cs]).then_inc(out_done, 16)
            sp.wait_ge(out_done, 16 * 2 * TT)

        def pool_block2(pool):
            pool.wait_ge(rows_free, 3 * DEPTH + 1)
            pool.dma_start(lnrow[:, 0, :], t["norm1_g_2"].partition_broadcast(P)).then_inc(ev["gain1_in"], 16)
            loads = [(amat[:, :, :], t["c_levels"]), (flip[:, :], t["c_flip"]),
                     (outg[:, 0:512], t["rec_out_g_2"].partition_broadcast(P)),
                     (outg[:, 512:], t["attn_out_g_2"].partition_broadcast(P)),
                     (small[:, :, :], t["w_in_2"].rearrange("o (k p) n -> p (o k) n", p=P)[:, :, 4096:4168])]
            loads += [(qkg[:, n, :], t[name].partition_broadcast(P)) for n, name in
                      enumerate(("q_norm_g_2", "k_norm_g_2", "idx_k_norm_g_2", "idx_k_norm_b_2"))]
            assert len(loads) == BLOCK2_LOADS
            for dst, src in loads:
                pool.dma_start(dst, src).then_inc(ev["block2_in"], 16)
            pool.wait_ge(ev["h1_free"], 1)
            pool.dma_start(lnrow[:, 0, :], t["norm2_g_2"].partition_broadcast(P)).then_inc(ev["gain2_in"], 16)
            pool.dma_start(table[:, 0:HANK], t["c_onehot"]).then_inc(ev["table_in"], 16)
            pool.dma_start(table[:, HANK:], t["rel_bias_2"]).then_inc(ev["table_in"], 16)
            pool.wait_ge(ev["rel_out"], 16)
            pool.wait_ge(ev["rec_in"], 1)
            sc = t["scratch"]
            pool.dma_start(hank[:, :, :], bass.AP(tensor=sc.tensor, offset=sc.offset, ap=[[1, P], [HANK, A_HEADS], [1, T]])
                           ).then_inc(ev["hank_in"], 16)
            pool.wait_ge(x_done, 4 * N_CAT + 4)
            pool.dma_start(rw[:, :, 0:4], t["w_rg_2"].rearrange("o (k p) n -> p (o k) n", p=P)).then_inc(ev["router_in"], 16)
            pool.dma_start(rw[:, :, 4:20], t["w_re_2"].rearrange("o (k p) n -> p (o k) n", p=P)).then_inc(ev["router_in"], 16)
            pool.dma_start(rbias[:, 0:4], t["b_rg_2"].partition_broadcast(P)).then_inc(ev["router_in"], 16)
            pool.dma_start(rbias[:, 4:20], t["b_re_2"].partition_broadcast(P)).then_inc(ev["router_in"], 16)

        def pe_block2(pe, cols_unit, tokens_unit, rows_unit, transpose_x, open_sums):
            mm = nc.tensor.matmul

            def mod_sums(r, b):
                for c in range(4):
                    last = mm(bank(b + c), ones[:, :], mod[:, r * 2048 + c * 512:r * 2048 + (c + 1) * 512],
                              start=True, stop=True)
                last.then_inc(ev[f"mod{r}_ps"], 1)

            pe.wait_ge(x_done, 12 * DEPTH + 4)
            mod_sums(0, 4)
            pe.wait_ge(ev["mod0"], 1)
            mod_sums(1, 4)
            transpose_x(N_H1, cat)
            pe.wait_ge(xTlo_done, 4 * N_H1 + 4)

            def level(n):
                pe.wait_ge(ev["lvl_ready"], n + 1)
                b = 4 + 2 * (n % 2)
                k, q = (kT, qT) if n == 0 else (kdT, qdT)
                if n == 0:
                    pe.wait_ge(ev["rel"], 1)
                elif n == 1:
                    pe.wait_ge(ev["ik_norm"], 1)
                for head in range(HEADS):
                    if n == LEVELS:
                        last = mm(bank(b, head * P, (head + 1) * P), k[:, head, 0:P], q[:, head, P:T], start=True, stop=True)
                        continue
                    for i in range(TT):
                        c = (head * 2 + i) * P
                        sl = slice(i * P, (i + 1) * P)
                        last = mm(banks(b, 2)[:, c:c + P], k[:, head, sl], q[:, head, sl], start=True, stop=True)
                last.then_inc(ev["lvl_ps"], 1)

            for u in range(16):
                if u >= EVAC_HOLD:
                    pe.wait_ge(ev["evac"], u - EVAC_HOLD + 1)
                b = u % EVAC_HOLD
                if u < 4 or u >= 14:
                    cols_unit(*at(BASE, u), xThi, xTlo, [bank(b, 0, T), bank(b, T)])
                else:
                    tokens_unit(*at(BASE, u), xThi, xTlo, b)
                if u == 0:
                    pe.wait_ge(ev["mod1"], 1)
                    mod_sums(2, 4)
                if u == 3:
                    pe.wait_ge(ev["mod2"], 1)
                    pe.wait_ge(ev["table_in"], 32)
                    mm(ps[0:A_HEADS, 5 * 512:5 * 512 + HANK], table[:, HANK:], table[:, 0:HANK], start=True,
                       stop=True).then_inc(ev["rel_ps"], 1)
                    pe.wait_ge(ev["block2_in"], 16 * BLOCK2_LOADS)
                    for i in range(TT):
                        for k in range(KD):
                            for part in range(2):
                                last = mm(bank(6 + i, 0, 72), hilo[part][:, k, i * P:(i + 1) * P], small[:, k, :],
                                          start=k == 0 and part == 0, stop=k == KD - 1 and part == 1)
                    last.then_inc(ev["ik_ps"], 1)
                if 5 <= u < 5 + LEVELS + 1:
                    level(u - 5)
                if u == 5 + LEVELS:
                    for i in range(TT):
                        last = nc.tensor.transpose(bank(5, i * P, (i + 1) * P), ikd[:, i, :], eye[:, :])
                    last.then_inc(ev["ikT_ps"], 1)
            pe.wait_ge(ev["rec_in"], 1)
            for head in range(HEADS):
                hs = slice(head * P, (head + 1) * P)
                mm(bank(6)[:, hs], amat[:, 2 * head, :], vtok[:, 0, hs], start=True, stop=True)
                mm(bank(7)[:, hs], amat[:, 2 * head + 1, :], vtok[:, 1, hs], start=True, stop=False)
                last = mm(bank(7)[:, hs], across[:, head, :], vtok[:, 0, hs], start=False, stop=True)
            last.then_inc(ev["recv_ps"], 1)

            def head_rows(h):
                return slice(64 * (h % 2), 64 * (h % 2) + 64)

            pe.wait_ge(ev["ikT"], 1)
            pe.wait_ge(ev["evac"], 16)
            for i in range(TT):
                for h in range(A_HEADS):
                    last = mm(spans(i)[:, pos(h), :], iqT[head_rows(h), h // 2, i * P:(i + 1) * P],
                              ikT[head_rows(h), 0:SPAN[i]], start=True, stop=True)
                last.then_inc(ev[f"sc{i}_ps"], 1)
            pe.wait_ge(ev["qk_norm"], 1)
            pe.wait_ge(ev["relu1"], 1)
            for i in range(TT):
                for k in range(8):
                    last = nc.tensor.transpose(xT_banks(i)[:, k, :], qk[:, i, k * P:(k + 1) * P], eye[:, :])
            last.then_inc(ev["qkT_ps"], 1)
            pe.wait_ge(ev["qkT"], 1)
            pe.wait_ge(ev["hank_in"], 16)
            for i in range(TT):
                pe.wait_ge(ev[f"relu{i}"], 1)
                for h in range(A_HEADS):
                    mm(spans(i)[:, pos(h), :], qkT[head_rows(h), h // 2, i * P:(i + 1) * P],
                       qkT[head_rows(h), 4 + h // 2, 0:SPAN[i]], start=True, stop=False)
                    last = mm(spans(i)[:, pos(h), :], flip[:, :], hank[:, h, T - SPAN[i]:T], start=False, stop=True)
                last.then_inc(ev[f"lg{i}_ps"], 1)
            for i in range(TT):
                pe.wait_ge(ev[f"exp{i}"], 1)
                if i == 0:
                    pe.wait_ge(ev["cat_rec"], 1)
                else:
                    pe.wait_ge(ev["araw"], 1)
                for kb in range(i + 1):
                    for h in range(A_HEADS):
                        c = (kb * A_HEADS + h) * P
                        last = nc.tensor.transpose(prob_banks(i)[:, c:c + P], logits(i)[:, h, kb * P:(kb + 1) * P], eye[:, :])
                last.then_inc(ev[f"lg_ps{i}"], 1)
                pe.wait_ge(ev[f"pT{i}"], 1)
                for h in range(A_HEADS):
                    for kb in range(i + 1):
                        last = mm(bank(AV_BANK[i], pos(h) * A_DH, (pos(h) + 1) * A_DH), pT[:, kb, pos(h), :],
                                  av[:, kb, h * A_DH:(h + 1) * A_DH], start=kb == 0, stop=kb == i)
                last.then_inc(ev[f"av{i}_ps"], 1)
            transpose_x(N_CAT, cat)
            pe.wait_ge(xTlo_done, 4 * N_CAT + 4)
            for q in range(4):
                rows_unit(*at(BASE, OFF_WOUT2 + q), xThi[:, 2 * q:2 * q + 2], xTlo[:, 2 * q:2 * q + 2], q == 0, q == 3)
            transpose_x(N_H2, cat)
            pe.wait_ge(xTlo_done, 4 * N_H2 + 4)
            pe.wait_ge(ev["rw_split"], 1)
            for k in range(KD):
                for j, (w, xp) in enumerate(((rwhi, xThi), (rwhi, xTlo), (rwlo, xThi))):
                    last = mm(ps[0:20, 4 * 512:4 * 512 + T], w[:, k, :], xp[:, k, :], start=k == 0 and j == 0,
                              stop=k == KD - 1 and j == 2)
            last.then_inc(ev["routeT_ps"], 1)
            pe.wait_ge(ev["routeT"], 1)
            for i in range(TT):
                last = nc.tensor.transpose(bank(5, i * 32, i * 32 + 20), rlogT[:, i * P:(i + 1) * P], eye[0:20, 0:20])
            last.then_inc(ev["route_ps"], 1)
            count = DEPTH * 2 * FFN_STEPS

            def gate_up(base, o, par):
                cols_unit(*at(base, o), xThi, xTlo, [bank(2 * par, 0, T), bank(2 * par + 1, 0, T)])
                cols_unit(*at(base, o + 1), xThi, xTlo, [bank(2 * par, T), bank(2 * par + 1, T)])

            def spread(experts, b):
                for j, e in enumerate(experts):
                    for i in range(TT):
                        c = b * 512 + j * T + i * P
                        ins = mm(ps[:, c:c + P], comb[:, i, e:e + 1].to_broadcast([P, P]), eye[:, :], start=True, stop=True)
                return ins

            gate_up(BASE, OFF_MOE, 0)
            pe.wait_ge(ev["comb"], 1)
            spread(range(0, 12), 2).then_inc(ev["comb_ps"], 1)
            pe.wait_ge(ev["comb_a"], 1)
            spread(range(12, 16), 2).then_inc(ev["comb_ps"], 1)
            pe.wait_ge(ev["comb_b"], 1)
            open_sums()
            pe.wait_ge(ev["comb_c"], 1)
            with pe.Fori(0, EXPERTS - 1) as i:
                for s in range(2):
                    o = OFF_MOE + 2 + 3 * s
                    gate_up(BASE + 2 * i, o, 1 - s)
                    pe.wait_ge(hlo_done, 2 * i + (count + s + 1))
                    rows_unit(*at(BASE + 2 * i, o + 2), hhi[:, s], hlo[:, s], False, False)
            o = OFF_MOE + 3 * MOE_STEPS - 4
            gate_up(BASE, o, 1)
            pe.wait_ge(hlo_done, count + MOE_STEPS - 1)
            rows_unit(*at(BASE, o + 2), hhi[:, 0], hlo[:, 0], False, False)
            pe.wait_ge(hlo_done, count + MOE_STEPS)
            rows_unit(*at(BASE, o + 3), hhi[:, 1], hlo[:, 1], False, True)

        def act_block2(act, turn, split_xT, silu, hid_hi):
            act_fn = nc.scalar.activation

            def rms_root(name):
                act_fn(spare[:, :], eps[:, 0:1], ACT.Sqrt)
                act.wait_ge(ev[f"ss{name}"], 1)
                act_fn(std[:, :, 0], var[:, :, 0], ACT.Sqrt).then_inc(ev[f"std{name}"], 1)

            act.wait_ge(ev["mod0_ps"], 1)
            act_fn(mod[:, 0:2048], banks(4, 4), ACT.Copy).then_inc(ev["mod0"], 1)
            rms_root("1")
            split_xT(N_H1)
            def root(dst, src, count, n, event):
                act_fn(nrm[:, dst, 0:count], nrm[:, src, 0:count], ACT.Sqrt, bias=eps[:, 1:2],
                       scale=1.0 / n).then_inc(ev[event], 1)

            for u in range(16):
                turn(BASE, u)
                src = halves(u % EVAC_HOLD)
                c = u % 2
                cs = slice(c * T, (c + 1) * T)
                if u < 2:
                    ins = act_fn(qT[:, 2 * c:2 * c + 2, :], src, ACT.Silu)
                elif u < 4:
                    ins = act_fn(fT[:, 2 * c:2 * c + 2, :], src, ACT.Tanh, scale=0.5)
                elif u < 6:
                    ins = act_fn(gate[:, :, cs], src, ACT.Silu)
                elif u < 8:
                    ins = act_fn(vtok[:, :, cs], src, ACT.Copy)
                elif u < 12:
                    o = (u - 8) * T
                    act_fn(qk[:, :, o:o + T], src, ACT.Copy)
                    if u == 8:
                        act.wait_ge(ev["rel_out"], 16)
                    elif u > 9:
                        act.wait_ge(ev["qk_ss"], u - 9)
                    ins = act_fn(squares[:, u % 2, :].rearrange("p (i c) -> p i c", i=TT), src, ACT.Square)
                elif u < 14:
                    ins = act_fn(av[:, :, cs], src, ACT.Copy)
                else:
                    ins = act_fn(iqT[:, 2 * c:2 * c + 2, :], src, ACT.Copy)
                ins.then_inc(ev["evac"], 1)
                if u == 1:
                    act.wait_ge(ev["mod2_ps"], 1)
                    act_fn(mod[:, 4096:6144], banks(4, 4), ACT.Copy).then_inc(ev["mod2"], 1)
                elif u == 3:
                    act.wait_ge(ev["rel_ps"], 1)
                    act_fn(relv, ps[0:A_HEADS, 5 * 512:5 * 512 + HANK], ACT.Copy).then_inc(ev["rel"], 1)
                    act.wait_ge(ev["rel"], 1)
                    act.dma_start(t["scratch"], relv).then_inc(ev["rel_out"], 16)
                elif u == 4:
                    act.wait_ge(ev["ik_mv"], 1)
                    act_fn(std[:, :, 0], mv[:, :, 1], ACT.Sqrt, bias=eps[:, 1:2]).then_inc(ev["ik_std"], 1)
                elif u == 12:
                    act.wait_ge(ev["qk_ss"], 4)
                    root(1, 0, 32, A_DH, "qk_std")
                elif u == 14:
                    act.wait_ge(ev["ikT_ps"], 1)
                    act_fn(ikT[:, :], bank(5, 0, T), ACT.Copy).then_inc(ev["ikT"], 1)

            act.wait_ge(ev["recv_ps"], 1)
            act_fn(cat[:, :, 512:], banks(6, 2).rearrange("p (i c) -> p i c", i=TT), ACT.Square).then_inc(ev["rec_sq"], 1)
            for i in range(TT):
                act.wait_ge(ev[f"sc{i}_ps"], 1)
                act_fn(logits(i), spans(i), ACT.Relu).then_inc(ev[f"relu{i}"], 1)
                if i == 0:
                    act.wait_ge(ev["rec_ss"], 1)
                    root(1, 0, 8, P, "rec_std")
            act.wait_ge(ev["qkT_ps"], 1)
            for i in range(TT):
                ins = act_fn(qkT[:, :, i * P:(i + 1) * P], xT_banks(i), ACT.Copy)
            ins.then_inc(ev["qkT"], 1)
            for i in range(TT):
                act.wait_ge(ev[f"lg{i}"], 1)
                for h in range(A_HEADS):
                    c = A_HEADS * i + h
                    ins = act_fn(logits(i)[:, h, :], logits(i)[:, h, :], ACT.Exp, bias=soft[:, 0, c:c + 1],
                                 accum_out=soft[:, 1, c:c + 1])
                ins.then_inc(ev[f"exp{i}"], 1)
                act.wait_ge(ev[f"lg_ps{i}"], 1)
                act_fn(pT[:, 0:i + 1].rearrange("p k h t -> p (k h t)"), prob_banks(i), ACT.Copy).then_inc(ev[f"pT{i}"], 1)
            act.wait_ge(ev["araw"], 2)
            lgf = lg[:, :, :].rearrange("p h s -> p (h s)")
            act_fn(lgf[:, 0:1024].rearrange("p (i c) -> p i c", i=TT), cat[:, :, 512:], ACT.Square).then_inc(ev["att_sq"], 1)
            act.wait_ge(ev["att_ss"], 1)
            root(1, 0, 16, A_DH, "att_std")
            split_xT(N_CAT)
            for q in range(3):
                turn(BASE, OFF_WOUT2 + q)
                if q == 1:
                    act.wait_ge(ev["router_in"], 64)
                    act_fn(rwhi[:, :, :], rw[:, :, :], ACT.Copy).then_inc(ev["rw_hi"], 1)
            rms_root("2")
            split_xT(N_H2)
            turn(BASE, OFF_WOUT2 + 3)
            act.wait_ge(ev["routeT_ps"], 1)
            act_fn(rlogT[:, :], ps[0:20, 4 * 512:4 * 512 + T], ACT.Copy).then_inc(ev["routeT"], 1)
            act.wait_ge(ev["rexp_in"], 1)
            act_fn(rt[:, :, 8:12], rt[:, :, 8:12], ACT.Exp).then_inc(ev["rexp"], 1)
            act.wait_ge(ev["rexp2_in"], 1)
            act_fn(rt[:, :, 32:33], rt[:, :, 32:33], ACT.Exp).then_inc(ev["rexp2"], 1)
            count = DEPTH * 2 * FFN_STEPS
            turn(BASE, OFF_MOE)
            silu(0, BASE, OFF_MOE + 1)
            act.wait_ge(ev["comb_ps"], 1)
            act_fn(cmb[:, 0:4, :].rearrange("p e t -> p (e t)"), banks(2, 2), ACT.Copy).then_inc(ev["comb_a"], 1)
            act.wait_ge(ev["comb_ps"], 2)
            act_fn(cmb[:, 12:16, :].rearrange("p e t -> p (e t)"), banks(2, 2), ACT.Copy).then_inc(ev["comb_c"], 1)
            hid_hi(0, count + 1)
            turn(BASE, OFF_MOE + 1)
            with act.Fori(0, EXPERTS - 1) as i:
                for s in range(2):
                    o, par = OFF_MOE + 2 + 3 * s, 1 - s
                    turn(BASE + 2 * i, o)
                    silu(par, BASE + 2 * i, o + 1)
                    hid_hi(par, 2 * i + (count + s + 2))
                    turn(BASE + 2 * i, o + 1)
                    turn(BASE + 2 * i, o + 2)
            last = UNITS - ROUND_2 * RING
            turn(BASE, last - 4)
            silu(1, BASE, last - 3)
            hid_hi(1, count + MOE_STEPS)

        def dve_block2(dve, pieces, turn, split_xT, hid_lo, refine):
            v = nc.vector

            def gain(r):
                v.tensor_scalar(lnrow[:, 1, :], row(mod, r), 1.0, None, ALU.add)

            def head_norms(count, n):
                v.tensor_scalar(nrm[:, 3, 0:count], nrm[:, 0, 0:count], 1.0 / n, RMS_EPS, ALU.mult, ALU.add)
                dve.drain()
                refine(nrm[:, 2, 0:count], nrm[:, 1, 0:count], nrm[:, 3, 0:count], newt[:, 0:count])

            def modulate(shift):
                refine(rstd[:, :, 0], std[:, :, 0], var[:, :, 0], newt[:, 0:TT])
                for i in range(TT):
                    v.scalar_tensor_tensor(cat[:, i, :], x[:, i, :], rstd[:, i, 0:1], lnrow[:, 0, :], ALU.mult, ALU.mult)
                    dve.drain()
                    v.tensor_tensor(cat[:, i, :], cat[:, i, :], lnrow[:, 1, :], ALU.mult)
                    dve.drain()
                    for cs in pieces(i):
                        v.tensor_tensor(cat[:, i, cs], cat[:, i, cs], row(mod, shift)[:, cs],
                                        ALU.add).then_inc(x_done, 2 - i)

            def square_stats(i):
                for n2 in range(2):
                    v.bn_stats(stats[:, i, n2, :], x[:, i, n2 * 512:(n2 + 1) * 512])

            def mean_squares(name):
                for i in range(TT):
                    v.bn_aggr(mv[:, i, :], stats[:, i, :, :].rearrange("p a b -> p (a b)"))
                dve.drain()
                v.tensor_tensor(var[:, :, 0], mv[:, :, 0], mv[:, :, 0], ALU.mult)
                dve.drain()
                v.scalar_tensor_tensor(var[:, :, 0], var[:, :, 0], RMS_EPS, mv[:, :, 1], ALU.add,
                                       ALU.add).then_inc(ev[f"ss{name}"], 1)

            for i in range(TT):
                square_stats(i)
            dve.drain()
            mean_squares("1")
            dve.wait_ge(ev["gain1_in"], 16)
            dve.wait_ge(ev["mod0"], 1)
            gain(1)
            dve.wait_ge(ev["std1"], 1)
            modulate(0)
            dve.drain()
            v.memset(tick[:, :], 0.0).then_inc(ev["h1_free"], 1)
            split_xT(N_H1)
            dve.wait_ge(ev["mod1_ps"], 1)
            v.tensor_copy(mod[:, 2048:4096], banks(4, 4)).then_inc(ev["mod1"], 1)
            for m, val in ((suf, 1.0), (qdT, 0.0), (kdT, 0.0)):
                v.memset(m[:, :, :], val)
            v.tensor_scalar(lbt[:, 3, :], lbt[:, 1, :], -1.0, None, ALU.mult)
            dve.wait_ge(ev["block2_in"], 16 * BLOCK2_LOADS)
            v.tensor_scalar(qkg[:, 0, :], qkg[:, 0, :], A_DH ** -0.5, None, ALU.mult)
            v.tensor_copy(levels[:, :, :], amat[:, :, :])
            dve.drain()
            v.memset(amat[:, :, :], 0.0)
            dve.drain()

            def select(n):
                b = 4 + 2 * (n % 2)
                v.copy_predicated(amat[:, :, :], levels[:, n:n + 1, :].to_broadcast([P, 2 * HEADS, P]),
                                  banks(b, 2).rearrange("p (m t) -> p m t", t=P))

            def decays(n):
                h = 2 ** (n - 1)
                q, k, f, s, qd, kd = (by_half(m, h) for m in (qT, kT, fT, suf, qdT, kdT))
                v.tensor_tensor(qd[:, :, 1, :], q[:, :, 1, :], f[:, :, 1, :], ALU.mult)
                v.tensor_tensor(kd[:, :, 0, :], k[:, :, 0, :], s[:, :, 0, :], ALU.mult)
                dve.drain()
                if n == LEVELS:
                    v.memset(tick[:, :], 0.0).then_inc(ev["lvl_ready"], 1)
                    return
                shape = [P, f.shape[1], h]
                v.tensor_tensor(s[:, :, 0, :], s[:, :, 0, :], f[:, :, 1, h - 1:h].to_broadcast(shape),
                                ALU.mult).then_inc(ev["lvl_ready"], 1)
                dve.drain()
                v.tensor_tensor(f[:, :, 1, :], f[:, :, 1, :], f[:, :, 0, h - 1:h].to_broadcast(shape), ALU.mult)
                dve.drain()

            for u in range(16):
                turn(BASE, u)
                n = u - 4
                if u == 3:
                    dve.wait_ge(ev["ik_ps"], 1)
                    for i in range(TT):
                        v.bn_stats(stats[:, i, 0, :], bank(6 + i, 0, A_DH))
                        v.tensor_scalar(iw[:, i, :], bank(6 + i, A_DH, 72), float(np.float32(A_HEADS ** -0.5)),
                                        A_DH ** -0.5, ALU.mult, ALU.mult)
                    dve.drain()
                    for i in range(TT):
                        ins = v.bn_aggr(mv[:, i, :], stats[:, i, 0, :])
                    ins.then_inc(ev["ik_mv"], 1)
                if n == 0:
                    dve.wait_ge(ev["evac"], 4)
                    for head in range(HEADS):
                        hs = slice(head, head + 1)
                        v.tensor_scalar(kT[:, head, :], fT[:, head, :], lbt[:, 3, hs], lbt[:, 1, hs], ALU.mult, ALU.add)
                    dve.drain()
                    for head in range(HEADS):
                        hs = slice(head, head + 1)
                        ins = v.tensor_scalar(fT[:, head, :], fT[:, head, :], lbt[:, 1, hs], lbt[:, 2, hs], ALU.mult, ALU.add)
                    ins.then_inc(ev["lvl_ready"], 1)
                    dve.drain()
                    dve.wait_ge(ev["ik_std"], 1)
                    v.tensor_scalar(var[:, :, 0], mv[:, :, 1], RMS_EPS, None, ALU.add)
                    dve.drain()
                    refine(rstd[:, :, 0], std[:, :, 0], var[:, :, 0], newt[:, 0:TT])
                    for i in range(TT):
                        v.tensor_scalar(ikd[:, i, 0:A_DH], bank(6 + i, 0, A_DH), mv[:, i, 0:1], rstd[:, i, 0:1],
                                        ALU.subtract, ALU.mult)
                    dve.drain()
                    for i in range(TT):
                        v.tensor_tensor(ikd[:, i, 0:A_DH], ikd[:, i, 0:A_DH], qkg[:, 2, :], ALU.mult)
                    dve.drain()
                    for i in range(TT):
                        v.tensor_tensor(ikd[:, i, 0:A_DH], ikd[:, i, 0:A_DH], qkg[:, 3, :], ALU.add)
                    dve.drain()
                    v.tensor_copy(ikd[:, :, A_DH:], ikd[:, :, 0:A_DH]).then_inc(ev["ik_norm"], 1)
                elif 0 < n <= LEVELS:
                    dve.wait_ge(ev["lvl_ps"], n)
                    select(n - 1)
                    decays(n)
                if 8 <= u < 12:
                    dve.wait_ge(ev["evac"], u + 1)
                    sums = nrm[:, 0, 0:32].rearrange("p (i m) -> p i m", i=TT)[:, :, 4 * (u - 8):4 * (u - 8) + 4]
                    v.tensor_reduce(sums, squares[:, u % 2, :].rearrange("p (i m c) -> p i m c", i=TT, c=A_DH), AX_X,
                                    ALU.add).then_inc(ev["qk_ss"], 1)
                elif u == 13:
                    dve.wait_ge(ev["qk_std"], 1)
                    head_norms(32, A_DH)
                    qkf = qk[:, :, :].rearrange("p i c -> p (i c)").rearrange("p (m c) -> p m c", c=A_DH)
                    v.tensor_tensor(qkf, qkf, nrm[:, 2, 0:32].unsqueeze(2).to_broadcast([P, 32, A_DH]), ALU.mult)
                elif u == 14:
                    dve.wait_ge(ev["lvl_ps"], LEVELS + 1)
                    v.tensor_copy(across[:, :, :].rearrange("p a t -> p (a t)"),
                                  bank(4 + 2 * (LEVELS % 2))).then_inc(ev["rec_in"], 1)
                    dve.drain()
                    for i in range(TT):
                        for half in range(2):
                            part = qkf[:, 16 * i + 8 * half:16 * i + 8 * half + 8, :]
                            ins = v.tensor_tensor(part, part, qkg[:, half:half + 1, :].to_broadcast([P, A_HEADS, A_DH]),
                                                  ALU.mult)
                    ins.then_inc(ev["qk_norm"], 1)
                    for i in range(TT):
                        v.tensor_tensor(gate[:, i, :], gate[:, i, :], outg[:, 0:512], ALU.mult)

            dve.wait_ge(ev["rec_sq"], 1)
            v.tensor_reduce(nrm[:, 0, 0:8].rearrange("p (i m) -> p i m", i=TT),
                            cat[:, :, 512:].rearrange("p i (m c) -> p i m c", c=P), AX_X, ALU.add).then_inc(ev["rec_ss"], 1)

            def choose(i):
                n = SPAN[i]
                rl, sc = logits(i), score[:, i, 0:n]
                dve.wait_ge(ev[f"relu{i}"], 1)
                for odd in range(2):
                    part = rl[:, 4 * odd:4 * odd + 4, :]
                    w = iw[:, i, :].rearrange("p (a b) -> p b a", b=2)[:, odd, :]
                    v.tensor_tensor(part, part, w.unsqueeze(2).to_broadcast([P, 4, n]), ALU.mult)
                dve.drain()
                v.tensor_reduce(sc, rl.rearrange("p (b a) s -> p s a b", b=2), AX_XY, ALU.add)
                dve.drain()
                v.memset(score[0:64, i, n - 64:n], -BIG)
                dve.drain()
                for _ in range(TOPK // 8):
                    v.max(top8[:, :], sc)
                    dve.drain()
                    v.match_replace(out=sc, in_to_replace=top8[:, :], in_values=sc, imm_value=-TAKEN)
                    dve.drain()
                v.tensor_scalar(sc, sc, -(BIG + TAKEN) / 2, -1.0e30, ALU.is_gt, ALU.mult)
                dve.drain()

            def mask(i):
                n = SPAN[i]
                cs = slice(A_HEADS * i, A_HEADS * i + A_HEADS)
                dve.wait_ge(ev[f"lg{i}_ps"], 1)
                v.tensor_tensor(logits(i), spans(i), score[:, i:i + 1, 0:n].to_broadcast([P, A_HEADS, n]), ALU.add)
                dve.drain()
                v.tensor_reduce(soft[:, 2, cs], logits(i), AX_X, ALU.max)
                dve.drain()
                v.tensor_scalar(soft[:, 0, cs], soft[:, 2, cs], -1.0, None, ALU.mult).then_inc(ev[f"lg{i}"], 1)

            def attended(i):
                cs = slice(A_HEADS * i, A_HEADS * i + A_HEADS)
                dve.wait_ge(ev[f"exp{i}"], 1)
                v.reciprocal(soft[:, 2, cs], soft[:, 1, cs])
                dve.drain()
                dve.wait_ge(ev[f"av{i}_ps"], 1)
                for odd in range(2):
                    ins = v.tensor_tensor(cat[:, i, 512:].rearrange("p (a b c) -> p b a c", b=2, c=A_DH)[:, odd],
                                          bank(AV_BANK[i], 256 * odd, 256 * odd + 256).rearrange("p (a c) -> p a c", c=A_DH),
                                          soft[:, 2, A_HEADS * i + 4 * odd:A_HEADS * i + 4 * odd + 4].unsqueeze(2)
                                          .to_broadcast([P, 4, A_DH]), ALU.mult)
                ins.then_inc(ev["araw"], 1)

            choose(0)
            dve.wait_ge(ev["rec_std"], 1)
            head_norms(8, P)
            for i in range(TT):
                v.tensor_tensor(cat[:, i, 0:512].rearrange("p (a c) -> p a c", c=P), bank(6 + i).rearrange("p (a c) -> p a c", c=P),
                                nrm[:, 2, 4 * i:4 * i + 4].unsqueeze(2).to_broadcast([P, HEADS, P]), ALU.mult)
            dve.drain()
            v.tensor_tensor(cat[:, :, 0:512], cat[:, :, 0:512], gate[:, :, :], ALU.mult).then_inc(ev["cat_rec"], 1)
            mask(0)
            choose(1)
            attended(0)
            mask(1)
            attended(1)
            lgf = lg[:, :, :].rearrange("p h s -> p (h s)")
            dve.wait_ge(ev["att_sq"], 1)
            v.tensor_reduce(nrm[:, 0, 0:16], lgf[:, 0:1024].rearrange("p (m c) -> p m c", c=A_DH), AX_X,
                            ALU.add).then_inc(ev["att_ss"], 1)
            dve.wait_ge(ev["att_std"], 1)
            head_norms(16, A_DH)
            for i in range(TT):
                att = cat[:, i, 512:].rearrange("p (h c) -> p h c", c=A_DH)
                v.tensor_tensor(att, att, nrm[:, 2, 8 * i:8 * i + 8].unsqueeze(2).to_broadcast([P, A_HEADS, A_DH]), ALU.mult)
            dve.drain()
            for i in range(TT):
                v.tensor_tensor(cat[:, i, 512:], cat[:, i, 512:], outg[:, 512:], ALU.mult).then_inc(x_done, 2)
            split_xT(N_CAT)
            for q in range(2):
                turn(BASE, OFF_WOUT2 + q)
                if q == 1:
                    dve.wait_ge(ev["rw_hi"], 1)
                    v.tensor_tensor(rwlo[:, :, :], rw[:, :, :], rwhi[:, :, :].bitcast(F32),
                                    ALU.subtract).then_inc(ev["rw_split"], 1)
            gain(4)
            dve.drain()
            dve.wait_ge(ev["gain2_in"], 16)
            v.tensor_tensor(lnrow[:, 1, :], lnrow[:, 1, :], lnrow[:, 0, :], ALU.mult)
            for i in range(TT):
                if i == 0:
                    dve.wait_ge(y0_done, 3 * DEPTH + 1)
                else:
                    dve.wait_ge(used, ROUND_2 * RING + OFF_MOE)
                v.tensor_tensor(cat[:, i, :], banks(4 + 2 * i, 2), row(mod, 2), ALU.mult)
                dve.drain()
                v.tensor_tensor(x[:, i, :], x[:, i, :], cat[:, i, :], ALU.add)
                dve.drain()
                square_stats(i)
            dve.drain()
            mean_squares("2")
            dve.wait_ge(ev["std2"], 1)
            refine(rstd[:, :, 0], std[:, :, 0], var[:, :, 0], newt[:, 0:TT])
            for i in range(TT):
                v.scalar_tensor_tensor(cat[:, i, :], x[:, i, :], rstd[:, i, 0:1], lnrow[:, 1, :], ALU.mult, ALU.mult)
                dve.drain()
                for cs in pieces(i):
                    v.tensor_tensor(cat[:, i, cs], cat[:, i, cs], row(mod, 3)[:, cs], ALU.add).then_inc(x_done, 2 - i)
            split_xT(N_H2)
            for q in (2, 3):
                turn(BASE, OFF_WOUT2 + q)

            def R(a, b):
                return rt[:, :, a:b]

            def first(eq, seen, dst):
                v.memset(R(seen, seen + 1), 0.0)
                v.tensor_copy(R(seen + 1, seen + 2), R(eq, eq + 1))
                dve.drain()
                for j in (2, 3):
                    v.tensor_tensor(R(seen + j, seen + j + 1), R(seen + j - 1, seen + j), R(eq + j - 1, eq + j), ALU.max)
                    dve.drain()
                v.tensor_tensor(R(dst, dst + 4), R(eq, eq + 4), R(seen, seen + 4), ALU.is_gt)
                dve.drain()

            def four(ap):
                return ap.to_broadcast([P, TT, 4])

            dve.wait_ge(ev["route_ps"], 1)
            for i in range(TT):
                v.tensor_tensor(rlog[:, i, :], bank(5, i * 32, i * 32 + 20), rbias[:, :], ALU.add)
            dve.drain()
            v.tensor_reduce(R(0, 1), rlog[:, :, 0:4], AX_X, ALU.max)
            dve.drain()
            v.tensor_tensor(R(4, 8), rlog[:, :, 0:4], four(R(0, 1)), ALU.is_equal)
            v.tensor_tensor(R(8, 12), rlog[:, :, 0:4], four(R(0, 1)), ALU.subtract).then_inc(ev["rexp_in"], 1)
            dve.drain()
            first(4, 12, 16)
            el = rlog[:, :, 4:20].rearrange("p i (g j) -> p i g j", j=4)
            tmp = R(36, 52).rearrange("p i (g j) -> p i g j", j=4)
            v.tensor_tensor(tmp, el, R(16, 20).unsqueeze(3).to_broadcast([P, TT, 4, 4]), ALU.mult)
            dve.drain()
            v.tensor_reduce(R(20, 24), tmp.rearrange("p i g j -> p i j g"), AX_X, ALU.add)
            dve.drain()
            v.tensor_reduce(R(1, 2), R(20, 24), AX_X, ALU.max)
            dve.drain()
            v.tensor_tensor(R(4, 8), R(20, 24), four(R(1, 2)), ALU.is_equal)
            dve.drain()
            first(4, 12, 24)
            v.tensor_scalar(R(52, 56), R(24, 28), -1.0e38, None, ALU.mult)
            dve.drain()
            v.tensor_tensor(R(20, 24), R(20, 24), R(52, 56), ALU.add)
            dve.drain()
            v.tensor_reduce(R(2, 3), R(20, 24), AX_X, ALU.max)
            dve.drain()
            v.tensor_tensor(R(32, 33), R(2, 3), R(1, 2), ALU.subtract).then_inc(ev["rexp2_in"], 1)
            v.tensor_tensor(R(4, 8), R(20, 24), four(R(2, 3)), ALU.is_equal)
            dve.drain()
            first(4, 12, 28)
            dve.wait_ge(ev["rexp"], 1)
            v.tensor_reduce(R(3, 4), R(8, 12), AX_X, ALU.add)
            dve.wait_ge(ev["rexp2"], 1)
            v.tensor_scalar(R(33, 34), R(32, 33), 1.0, None, ALU.add)
            dve.drain()
            v.reciprocal(R(3, 4), R(3, 4))
            v.reciprocal(R(33, 34), R(33, 34))
            dve.drain()
            v.tensor_tensor(R(34, 35), R(32, 33), R(33, 34), ALU.mult)
            dve.drain()
            v.tensor_tensor(R(33, 35), R(33, 35), R(3, 4).to_broadcast([P, TT, 2]), ALU.mult)
            dve.drain()
            v.tensor_tensor(R(24, 28), R(24, 28), four(R(33, 34)), ALU.mult)
            v.tensor_tensor(R(28, 32), R(28, 32), four(R(34, 35)), ALU.mult)
            dve.drain()
            v.tensor_tensor(R(24, 28), R(24, 28), R(28, 32), ALU.add)
            dve.drain()
            for g in range(4):
                ins = v.tensor_tensor(comb[:, :, 4 * g:4 * g + 4], R(24, 28), four(R(16 + g, 17 + g)), ALU.mult)
            ins.then_inc(ev["comb"], 1)
            count = DEPTH * 2 * FFN_STEPS

            def hidden(par, expert, n):
                dve.wait_ge(silu_done, n)
                v.tensor_tensor(sil[:, :, :], sil[:, :, :], cmb[:, bass.ds(expert, 1), :].to_broadcast([P, 2, T]), ALU.mult)
                dve.drain()
                up = banks(2 * par, 2).rearrange("p (c u t) -> p c u t", u=2, t=T)[:, :, 1, :]
                v.tensor_tensor(hid[:, par], sil[:, :, :], up, ALU.mult).then_inc(hid_done, 1)

            turn(BASE, OFF_MOE)
            dve.wait_ge(ev["comb_ps"], 1)
            v.tensor_copy(cmb[:, 4:12, :].rearrange("p e t -> p (e t)"), banks(4, 4)).then_inc(ev["comb_b"], 1)
            dve.wait_ge(ev["comb_a"], 1)
            hidden(0, 0, count + 1)
            hid_lo(0, count + 1)
            turn(BASE, OFF_MOE + 1)
            dve.wait_ge(ev["comb_c"], 1)
            with dve.Fori(0, EXPERTS - 1) as i:
                for s in range(2):
                    o, par = OFF_MOE + 2 + 3 * s, 1 - s
                    turn(BASE + 2 * i, o)
                    hidden(par, i + s, 2 * i + (count + s + 2))
                    hid_lo(par, 2 * i + (count + s + 2))
                    turn(BASE + 2 * i, o + 1)
                    turn(BASE + 2 * i, o + 2)
            turn(BASE, UNITS - ROUND_2 * RING - 4)
            hidden(1, EXPERTS - 1, count + MOE_STEPS)
            hid_lo(1, count + MOE_STEPS)
            for i in range(TT):
                if i == 0:
                    dve.wait_ge(y0_done, 3 * DEPTH + 2)
                else:
                    dve.wait_ge(used, UNITS)
                for half in range(2):
                    cs = slice(512 * half, 512 * half + 512)
                    v.tensor_tensor(lnrow[:, i, cs], bank(4 + 2 * i + half), row(mod, 5)[:, cs], ALU.mult)
                    dve.drain()
                    v.tensor_tensor(x[:, i, cs], x[:, i, cs], lnrow[:, i, cs], ALU.add).then_inc(ev["final"], 1)

        def proj_bank(name, a):
            return PROJ_UNITS.index((name, a)) % 4

        def proj(name, a):
            b = proj_bank(name, a)
            return halves(b), bank_free[b]

        block = ctx.enter_context(nc.Block())

        def unit_no(rnd, slot):
            return rnd * RING + slot

        @block.sync
        def _(sp):
            def load(rnd, slot):
                sp.wait_ge(lo_done, unit_no(rnd, slot) + 1)
                sp.dma_start(raw[:, slot, :], t["stream"][bass.ds(unit_no(rnd, slot), 1), :, :].rearrange(
                    "o p n -> p (o n)")).then_inc(loaded[slot], 16)

            sp.dma_start(eye[:, :], t["c_eye"]).then_inc(eye_in, 16)
            sp.dma_start(x[:, :, :], t["x"].rearrange("o (i p) d -> p (o i) d", p=P)).then_inc(x_in, 16)
            with sp.Fori(0, UNITS // RING) as rnd:
                for slot in range(RING):
                    load(rnd, slot)
            for slot in range(UNITS % RING):
                load(UNITS // RING, slot)
            sp_block2(sp)

        @block.gpsimd
        def _(pool):
            for l in range(DEPTH):
                for v, name, n in ((V_SC, "sc_w", 3), (V_RC, "rc_w", 4), (V_RCB, "rc_b", 1), (V_BM, "b_merge", 2),
                                   (V_RGB, "rg_b", 2), (V_A, "a_param", 1)):
                    src = t[name][l:l + 1]
                    src = src.rearrange("o g (k c) -> (o g k) c", c=P) if len(src.shape) == 3 \
                        else src.rearrange("o (k c) -> (o k) c", c=P)
                    pool.dma_start(vrows[v * KD:(v + n) * KD, l, :], src).then_inc(const_in, 16)
            pool.dma_start(crows[0:KD, :], t["c_2"].rearrange("o (k c) -> (o k) c", c=P)).then_inc(const_in, 16)
            pool.dma_start(crows[KD:2 * KD, :], t["lb_logits_2"].rearrange("o (k c) -> (o k) c", c=P)).then_inc(const_in, 16)
            pool.wait_ge(setup_dve, 1)
            pool.dma_start(mod[0:1, :], t["b_ada_2"]).then_inc(bada_in, 16)
            lg3 = t["ln_g"].rearrange("l n d -> (l n) d")
            lb3 = t["ln_b"].rearrange("l n d -> (l n) d")

            def norm_rows(n):
                pool.wait_ge(rows_free, n + 1)
                pool.dma_start(lnrow[:, 0, :], lg3[bass.ds(n, 1), :].partition_broadcast(P)).then_inc(rows_in, 16)
                pool.dma_start(lnrow[:, 1, :], lb3[bass.ds(n, 1), :].partition_broadcast(P)).then_inc(rows_in, 16)

            with pool.Fori(0, DEPTH) as l:
                norm_rows(l * 3)
                norm_rows(l * 3 + 1)
                for i in range(ADA_PIECES):
                    if i < 2:
                        pool.wait_ge(yblo_done, l * 2 + 3)
                    else:
                        pool.wait_ge(ada_used, l * ADA_PIECES + (i - 1))
                    pool.dma_start(adaraw[:, i % 2, :], t["ada"][bass.ds(l * ADA_PIECES + i, 1), :, :].rearrange(
                        "o p n -> p (o n)")).then_inc(ada_in[i % 2], 16)
                norm_rows(l * 3 + 2)
            pool_block2(pool)

        @block.tensor
        def _(pe):
            def weights_ready(rnd, slot):
                pe.wait_ge(lo_done, unit_no(rnd, slot) + 1 + RING)

            def cols_unit(rnd, slot, xh, xl, outs):
                weights_ready(rnd, slot)
                for tile in range(2):
                    for k in range(KD):
                        c = k * 256 + tile * P
                        wh, wl = whi[:, slot, c:c + P], wlo[:, slot, c:c + P]
                        nc.tensor.matmul(outs[tile], wh, xh[:, k, :], start=k == 0, stop=False)
                        nc.tensor.matmul(outs[tile], wh, xl[:, k, :], start=False, stop=False)
                        last = nc.tensor.matmul(outs[tile], wl, xh[:, k, :], start=False, stop=k == KD - 1)
                last.then_inc(used, 1)

            def tokens_unit(rnd, slot, xh, xl, b):
                weights_ready(rnd, slot)
                for i in range(TT):
                    o = bank(b, i * T, (i + 1) * T)
                    for k in range(KD):
                        wh, wl = whi[:, slot, k * 256:(k + 1) * 256], wlo[:, slot, k * 256:(k + 1) * 256]
                        h, lo = xh[:, k, i * P:(i + 1) * P], xl[:, k, i * P:(i + 1) * P]
                        nc.tensor.matmul(o, h, wh, start=k == 0, stop=False)
                        nc.tensor.matmul(o, h, wl, start=False, stop=False)
                        last = nc.tensor.matmul(o, lo, wh, start=False, stop=k == KD - 1)
                last.then_inc(used, 1)

            def rows_unit(rnd, slot, hh, hl, start, stop):
                weights_ready(rnd, slot)
                for i in range(TT):
                    for k in range(2):
                        h, lo = hh[:, k, i * P:(i + 1) * P], hl[:, k, i * P:(i + 1) * P]
                        for n in range(2):
                            c = k * D + n * 512
                            o = bank(4 + 2 * i + n)
                            nc.tensor.matmul(o, h, whi[:, slot, c:c + 512], start=start and k == 0, stop=False)
                            nc.tensor.matmul(o, h, wlo[:, slot, c:c + 512], start=False, stop=False)
                        for n in range(2):
                            c = k * D + n * 512
                            last = nc.tensor.matmul(bank(4 + 2 * i + n), lo, whi[:, slot, c:c + 512],
                                                    start=False, stop=stop and k == 1)
                    if stop and i == 0:
                        last.then_inc(y0_done, 1)
                last.then_inc(used, 1)

            def transpose_x(n, src):
                for i in range(TT):
                    for b in range(2):
                        pe.wait_ge(x_done, n * 4 + (2 * i + b + 1))
                        for k in range(4 * b, 4 * b + 4):
                            last = nc.tensor.transpose(xT_banks(i)[:, k, :], src[:, i, k * P:(k + 1) * P], eye[:, :])
                        last.then_inc(xT_ps, 1)

            def open_sums():
                for b in range(4, 8):
                    nc.tensor.matmul(bank(b), zero_w[:, :], xThi[:, 0:2, :].rearrange("p k t -> p (k t)"),
                                     start=True, stop=False)

            def ffn(base, f, n):
                pe.wait_ge(xTlo_done, n * 4 + 4)
                cols_unit(*at(base, 0), xThi, xTlo, [bank(0, 0, T), bank(1, 0, T)])
                cols_unit(*at(base, 1), xThi, xTlo, [bank(0, T), bank(1, T)])
                pe.wait_ge(setup_dve, 2)
                open_sums()
                with pe.Fori(0, FFN_STEPS // 2) as i:
                    for s in range(2):
                        o, par = 2 + 3 * s, 1 - s
                        cols_unit(*at(base + 2 * i, o), xThi, xTlo, [bank(2 * par, 0, T), bank(2 * par + 1, 0, T)])
                        cols_unit(*at(base + 2 * i, o + 1), xThi, xTlo, [bank(2 * par, T), bank(2 * par + 1, T)])
                        pe.wait_ge(hlo_done, f * FFN_STEPS + 2 * i + s + 1)
                        rows_unit(*at(base + 2 * i, o + 2), hhi[:, 1 - par], hlo[:, 1 - par], False, False)
                pe.wait_ge(hlo_done, (f + 1) * FFN_STEPS)
                rows_unit(*at(base, UNITS_FFN - 1), hhi[:, 0], hlo[:, 0], False, True)

            pe.wait_ge(eye_in, 16)
            transpose_x(0, x)
            pe.wait_ge(const_in, 16 * NCONST)
            for l in range(DEPTH):
                nc.tensor.transpose(bank(4 + l, 0, NVEC * KD), vrows[:, l, :], eye[0:NVEC * KD, 0:NVEC * KD])
            nc.tensor.transpose(bank(6, 0, 2 * KD), crows[:, :], eye[0:2 * KD, 0:2 * KD]).then_inc(setup_pe, 1)

            with pe.Fori(0, DEPTH) as l:
                lay = l * ROUNDS_LAYER
                ffn(lay, l * 2, l * 3)
                transpose_x(l * 3 + 1, x)
                with pe.Fori(0, 2) as hf:
                    pe.wait_ge(xTlo_done, l * 12 + 8)
                    base = lay + OFF_MIX // RING + hf * (UNITS_HALF // RING)
                    g = l * 2 + hf
                    for u, unit in enumerate(HALF):
                        rnd, slot = at(base, u)
                        if unit in PROJ_UNITS:
                            j = PROJ_UNITS.index(unit)
                            b = j % 4
                            pe.wait_ge(bank_free[b], g * BANK_USES[b] + (j // 4 + 1))
                            cols_unit(rnd, slot, xThi, xTlo, [bank(b, 0, T), bank(b, T)])
                            continue
                        pe.wait_ge(xclo_done, g * 2 + 2)
                        pe.wait_ge(gates_read, g + 1)
                        weights_ready(rnd, slot)
                        for gt in range(2):
                            for a in range(2):
                                for jt in range(2):
                                    o = halves(4, 4)[:, gt * 4 + a * 2 + jt, :]
                                    for k in range(2):
                                        c = ((gt * 2 + a) * 2 + k) * 256 + jt * P
                                        wh, wl = whi[:, slot, c:c + P], wlo[:, slot, c:c + P]
                                        nc.tensor.matmul(o, wh, xchi[:, 2 * a + k, :], start=k == 0, stop=False)
                                        nc.tensor.matmul(o, wh, xclo[:, 2 * a + k, :], start=False, stop=False)
                                        last = nc.tensor.matmul(o, wl, xchi[:, 2 * a + k, :], start=False, stop=k == 1)
                        last.then_inc(used, 1)
                base = lay + OFF_MERGE // RING
                for i, (kind, q) in enumerate(MERGE):
                    if kind == "conv":
                        pe.wait_ge(yalo_done, l * 4 + 4)
                        pe.wait_ge(bank_free[q], (l * 2 + 2) * BANK_USES[q] + 1)
                        cols_unit(*at(base, i), yahi, yalo, [bank(q, 0, T), bank(q, T)])
                    elif kind == "rnn":
                        pe.wait_ge(yblo_done, l * 2 + 3)
                        pe.wait_ge(merged, l * 8 + q + 1)
                        cols_unit(*at(base, i), ybhi, yblo, [bank(q, 0, T), bank(q, T)])
                    else:
                        pe.wait_ge(mlo_done, l * 4 + q + 1)
                        rows_unit(*at(base, i), xThi[:, 2 * q:2 * q + 2], xTlo[:, 2 * q:2 * q + 2], q == 0, q == 3)
                transpose_x(l * 3 + 2, x)
                ffn(lay + OFF_FFN2 // RING, l * 2 + 1, l * 3 + 2)
                transpose_x(l * 3 + 3, x)
            pe_block2(pe, cols_unit, tokens_unit, rows_unit, transpose_x, open_sums)

        @block.scalar
        def _(act):
            act_fn = nc.scalar.activation

            def split(rnd, slot, first=False):
                if not first:
                    act.wait_ge(used, unit_no(rnd, slot) - RING + 1)
                act.wait_ge(loaded[slot], rnd * 16 + 16)
                act_fn(whi[:, slot, :], raw[:, slot, :], ACT.Copy).then_inc(hi_done, 1)

            def turn(base, o):
                split(*at(base, o + RING))

            def split_xT(n):
                for i in range(TT):
                    for b in range(2):
                        act.wait_ge(xT_ps, n * 4 + (2 * i + b + 1))
                        ks = slice(4 * b, 4 * b + 4)
                        act_fn(xThi[:, ks, i * P:(i + 1) * P], xT_banks(i)[:, ks, :], ACT.Copy).then_inc(xThi_done, 1)

            def silu(par, base, o):
                act.wait_ge(used, unit_no(*at(base, o)) + 1)
                src = banks(2 * par, 2).rearrange("p (c u t) -> p c u t", u=2, t=T)[:, :, 0, :]
                act_fn(sil[:, :, :], src, ACT.Silu).then_inc(silu_done, 1)

            def hid_hi(par, count):
                act.wait_ge(hid_done, count)
                act_fn(hhi[:, par], hid[:, par], ACT.Copy).then_inc(hhi_done, 1)

            def norm(n):
                act_fn(spare[:, :], eps[:, 0:1], ACT.Sqrt)
                act.wait_ge(mv_done, n + 1)
                act_fn(std[:, :, 0], mv[:, :, 1], ACT.Sqrt, bias=eps[:, 0:1]).then_inc(std_done, 1)

            def ffn(base, f):
                turn(base, 0)
                silu(0, base, 1)
                hid_hi(0, f * FFN_STEPS + 1)
                turn(base, 1)
                with act.Fori(0, FFN_STEPS // 2) as i:
                    for s in range(2):
                        o, par = 2 + 3 * s, 1 - s
                        turn(base + 2 * i, o)
                        silu(par, base + 2 * i, o + 1)
                        hid_hi(par, f * FFN_STEPS + 2 * i + s + 2)
                        turn(base + 2 * i, o + 1)
                        turn(base + 2 * i, o + 2)

            split_xT(0)
            for slot in range(RING):
                split(0, slot, first=True)
            act.wait_ge(setup_dve, 3)
            act_fn(spt[:, 1, :], spt[:, 0, :], ACT.Exp, scale=-1.0).then_inc(setup_act, 1)
            act_fn(lbt[:, 3:5, :], lbt[:, 1:3, :], ACT.Exp).then_inc(setup_act, 1)
            act_fn(csil[:, :], cvec[:, 0, :], ACT.Tanh, scale=0.5).then_inc(setup_act, 1)
            with act.Fori(0, DEPTH) as l:
                lay = l * ROUNDS_LAYER
                ffn(lay, l * 2)
                norm(l * 3)
                split_xT(l * 3 + 1)
                turn(lay, UNITS_FFN - 1)
                with act.Fori(0, 2) as hf:
                    base = lay + OFF_MIX // RING + hf * (UNITS_HALF // RING)
                    g = l * 2 + hf
                    act.wait_ge(half_start, g + 1)
                    act.wait_ge(yblo_done, g + 1)
                    for u, (name, a) in enumerate(HALF):
                        turn(base, u)
                        if name == "gates":
                            for c in range(4):
                                act_fn(tt_[:, c, :], halves(4, 4)[:, 4 + c, :], ACT.Tanh, bias=now[:, V_RGB + 1, c:c + 1],
                                       scale=0.5)
                            act.drain()
                            for c in range(4):
                                ins = act_fn(tt_[:, c, :], tt_[:, c, :], ACT.Tanh, bias=now[:, V_A, c:c + 1],
                                             scale=now[:, V_A, c:c + 1])
                            ins.then_inc(t_done, 1)
                            for c in range(4):
                                ins = act_fn(gin[:, c, :], halves(4, 4)[:, c, :], ACT.Tanh, bias=now[:, V_RGB, c:c + 1],
                                             scale=0.5)
                            ins.then_inc(gates_read, 1)
                            act.wait_ge(t_read, g + 1)
                            act_fn(tt_[:, :, :], tt_[:, :, :], ACT.Sqrt).then_inc(sqrt_done, 1)
                            continue
                        hd = g * 2 + a
                        kt = bass.ds(hf * 4 + 2 * a, 2)
                        two = slice(2 * a, 2 * a + 2)
                        src, free = proj(name, a)
                        if name == "x_r":
                            act.wait_ge(xc_done, hd + 1)
                            act_fn(xrp[:, :, 3:], src, ACT.Copy).then_inc(free, 1)
                            act.drain()
                            for jt in range(2):
                                c = 2 * a + jt
                                ins = act_fn(xc[:, c, :], xrp[:, jt, 0:T], ACT.Identity,
                                             bias=now[:, V_RCB, c:c + 1], scale=now[:, V_RC, c:c + 1])
                            ins.then_inc(xc_part, 1)
                            act.wait_ge(xc_done, hd + 2)
                            act_fn(xchi[:, two, :], xc[:, two, :], ACT.Copy).then_inc(xchi_done, 1)
                        elif name == "y_r":
                            act_fn(gel[:, two, :], src, ACT.Gelu_apprx_tanh).then_inc(free, 1)
                        elif name == "c_gate":
                            act.wait_ge(cv_part, hd + 1)
                            act_fn(zpad[:, :, 2:], src, ACT.Copy).then_inc(free, 1)
                        elif name == "v" and a == 1:
                            act.wait_ge(yb_done, g + 1)
                            act_fn(ybhi[:, bass.ds(hf * 4, 4), :], gel[:, :, :], ACT.Copy).then_inc(ybhi_done, 1)
                        elif name == "b_gate":
                            act.wait_ge(cv_done, hd + 1)
                            act_fn(yahi[:, kt, :], cv[:, :, :], ACT.Copy).then_inc(yahi_done, 1)
                        elif name in ("g_a", "g_b"):
                            dst, vec = (ga, V_BM) if name == "g_a" else (gb, V_BM + 1)
                            for jt in range(2):
                                c = 2 * a + jt
                                ins = act_fn(dst[:, bass.ds(hf * 4 + c, 1), :].rearrange("p o t -> p (o t)"),
                                             src[:, jt, :], ACT.Tanh, bias=now[:, vec, c:c + 1], scale=0.5)
                            ins.then_inc(free, 1)
                base = lay + OFF_MERGE // RING
                for i, (kind, q) in enumerate(MERGE):
                    if i < UNITS_MERGE - 1:
                        turn(base, i)
                    if kind == "rnn":
                        act.wait_ge(m_done, l * 4 + q + 1)
                        act_fn(xThi[:, 2 * q:2 * q + 2, :], ga[:, 2 * q:2 * q + 2, :], ACT.Copy, scale=0.5).then_inc(mhi_done, 1)
                norm(l * 3 + 1)
                split_xT(l * 3 + 2)
                turn(base, UNITS_MERGE - 1)
                ffn(lay + OFF_FFN2 // RING, l * 2 + 1)
                norm(l * 3 + 2)
                split_xT(l * 3 + 3)
                turn(lay + OFF_FFN2 // RING, UNITS_FFN - 1)
            act_block2(act, turn, split_xT, silu, hid_hi)

        @block.vector
        def _(dve):
            v = nc.vector

            def refine(r, root, var, t):
                v.reciprocal(r, root)
                dve.drain()
                v.tensor_tensor(t, r, r, ALU.mult)
                dve.drain()
                v.tensor_tensor(t, t, var, ALU.mult)
                dve.drain()
                v.tensor_scalar(t, t, -0.5, 1.5, ALU.mult, ALU.add)
                dve.drain()
                v.tensor_tensor(r, r, t, ALU.mult)
                dve.drain()

            def split(rnd, slot):
                dve.wait_ge(hi_done, unit_no(rnd, slot) + 1)
                v.tensor_tensor(wlo[:, slot, :], raw[:, slot, :], whi[:, slot, :].bitcast(F32),
                                ALU.subtract).then_inc(lo_done, 1)

            def turn(base, o):
                split(*at(base, o + RING))

            def split_xT(n):
                for i in range(TT):
                    for b in range(2):
                        dve.wait_ge(xThi_done, n * 4 + (2 * i + b + 1))
                        ks, sl = slice(4 * b, 4 * b + 4), slice(i * P, (i + 1) * P)
                        v.tensor_tensor(xTlo[:, ks, sl], xT_banks(i)[:, ks, :], xThi[:, ks, sl].bitcast(F32),
                                        ALU.subtract).then_inc(xTlo_done, 1)

            def hidden(par, count):
                dve.wait_ge(silu_done, count)
                up = banks(2 * par, 2).rearrange("p (c u t) -> p c u t", u=2, t=T)[:, :, 1, :]
                v.scalar_tensor_tensor(hid[:, par], sil[:, :, :], 0.5, up, ALU.mult, ALU.mult).then_inc(hid_done, 1)

            def hid_lo(par, count):
                dve.wait_ge(hhi_done, count)
                v.tensor_tensor(hlo[:, par], hid[:, par], hhi[:, par].bitcast(F32), ALU.subtract).then_inc(hlo_done, 1)

            def pieces(i):
                return [slice(0, D)] if i == 0 else [slice(0, 512), slice(512, D)]

            def norm(n, units):
                for i in range(TT):
                    if i == 0:
                        dve.wait_ge(y0_done, n + 1)
                    else:
                        dve.wait_ge(used, units)
                    v.scalar_tensor_tensor(x[:, i, :], x[:, i, :], ALPHA, banks(4 + 2 * i, 2), ALU.mult, ALU.add)
                    dve.drain()
                    for n2 in range(2):
                        v.bn_stats(stats[:, i, n2, :], x[:, i, n2 * 512:(n2 + 1) * 512])
                    dve.drain()
                    ins = v.bn_aggr(mv[:, i, :], stats[:, i, :, :].rearrange("p a b -> p (a b)"))
                ins.then_inc(mv_done, 1)
                dve.drain()
                dve.wait_ge(rows_in, n * 32 + 32)
                v.tensor_scalar(var[:, :, 0], mv[:, :, 1], LN_EPS, None, ALU.add)
                for i in range(TT):
                    v.scalar_tensor_tensor(x[:, i, :], x[:, i, :], mv[:, i, 0:1], lnrow[:, 0, :], ALU.subtract, ALU.mult)
                    if i == 0:
                        dve.drain()
                        dve.wait_ge(std_done, n + 1)
                        refine(rstd[:, :, 0], std[:, :, 0], var[:, :, 0], newt[:, 0:TT])
                    else:
                        dve.drain()
                    for cs in pieces(i):
                        v.scalar_tensor_tensor(x[:, i, cs], x[:, i, cs], rstd[:, i, 0:1], lnrow[:, 1, cs], ALU.mult,
                                               ALU.add).then_inc(x_done, 2 - i)
                dve.drain()
                v.memset(tick[:, :], 0.0).then_inc(rows_free, 1)

            def ada_piece(l, piece, parity, before):
                dve.drain()
                dve.wait_ge(ada_in[parity], l * (16 * ADA_PIECES // 2) + before * 16 + 16)
                part = mod[:, bass.ds(piece * 512, 512)]
                for k in range(KD // DEPTH):
                    v.scalar_tensor_tensor(part, adaraw[:, parity, k * 512:(k + 1) * 512], csil_now[:, k:k + 1],
                                                 part, ALU.mult, ALU.add)
                    dve.drain()
                v.memset(tick[:, :], 0.0).then_inc(ada_used, 1)

            def ffn(base, f, ada_layer=None):
                turn(base, 0)
                hidden(0, f * FFN_STEPS + 1)
                hid_lo(0, f * FFN_STEPS + 1)
                if ada_layer is not None:
                    for piece in range(2):
                        ada_piece(ada_layer, piece, piece, 0)
                with dve.Fori(0, FFN_STEPS // 2) as i:
                    for s in range(2):
                        o, par = 2 + 3 * s, 1 - s
                        turn(base + 2 * i, o - 1)
                        turn(base + 2 * i, o)
                        if ada_layer is not None:
                            ada_piece(ada_layer, 2 * i + (s + 2), s, i + 1)
                        hidden(par, f * FFN_STEPS + 2 * i + s + 2)
                        hid_lo(par, f * FFN_STEPS + 2 * i + s + 2)
                        turn(base + 2 * i, o + 1)

            v.memset(zero_w[:, :].bitcast(F32), 0.0)
            v.memset(ones[:, :], 1.0)
            v.memset(eps[:, 0:1], LN_EPS)
            v.memset(eps[:, 1:2], RMS_EPS)
            v.memset(mod[:, :], 0.0).then_inc(setup_dve, 1)
            dve.sem_inc(lo_done, RING)
            for free in (*bank_free, gates_read, rows_free, yblo_done, xc_done, cv_part):
                dve.sem_inc(free, 1)
            dve.wait_ge(x_in, 16)
            dve.sem_inc(x_done, 4)
            split_xT(0)
            for slot in range(RING):
                split(0, slot)
            dve.wait_ge(setup_pe, 1)
            for l in range(DEPTH):
                v.tensor_copy(vecs[:, l].rearrange("p v h k -> p (v h k)"), bank(4 + l, 0, NVEC * KD))
            v.tensor_copy(cvec[:, :, :].rearrange("p a k -> p (a k)"), bank(6, 0, 2 * KD))
            dve.drain()
            v.memset(tick[:, :], 0.0).then_inc(setup_dve, 1)
            for l in range(DEPTH):
                half = vecs[:, l, V_BM:V_A].rearrange("p v h k -> p (v h k)")
                v.tensor_scalar(half, half, 0.5, None, ALU.mult)
                v.tensor_copy(spt[:, 4, l * KD:(l + 1) * KD], vecs[:, l, V_A].rearrange("p h k -> p (h k)"))
            v.tensor_tensor(lbt[:, 0, :], cvec[:, 1, 0:4], cvec[:, 1, 4:8], ALU.max)
            dve.drain()
            v.tensor_scalar(spt[:, 0, :], spt[:, 4, :], -1.0, None, ALU.mult)
            v.tensor_tensor(lbt[:, 1, :], cvec[:, 1, 0:4], lbt[:, 0, :], ALU.subtract)
            v.tensor_tensor(lbt[:, 2, :], cvec[:, 1, 4:8], lbt[:, 0, :], ALU.subtract)
            dve.drain()
            v.tensor_tensor(spt[:, 0, :], spt[:, 4, :], spt[:, 0, :], ALU.max).then_inc(setup_dve, 1)
            dve.wait_ge(setup_act, 2)
            v.tensor_scalar(spt[:, 2, :], spt[:, 1, :], 2.0, None, ALU.add)
            dve.drain()
            v.reciprocal(spt[:, 2, :], spt[:, 2, :])
            dve.drain()
            v.tensor_tensor(spt[:, 1, :], spt[:, 1, :], spt[:, 2, :], ALU.mult)
            dve.drain()
            v.tensor_tensor(spt[:, 2, :], spt[:, 1, :], spt[:, 1, :], ALU.mult)
            v.memset(spt[:, 3, :], 1.0 / 17)
            dve.drain()
            for odd in (15, 13, 11, 9, 7, 5, 3, 1):
                v.tensor_tensor(spt[:, 3, :], spt[:, 3, :], spt[:, 2, :], ALU.mult)
                dve.drain()
                v.tensor_scalar(spt[:, 3, :], spt[:, 3, :], 1.0 / odd, None, ALU.add)
                dve.drain()
            v.tensor_tensor(spt[:, 3, :], spt[:, 3, :], spt[:, 1, :], ALU.mult)
            v.tensor_scalar(spt[:, 4, :], spt[:, 4, :], -1.0, 0.0, ALU.mult, ALU.max)
            dve.drain()
            v.tensor_scalar(spt[:, 4, :], spt[:, 4, :], 2.0, None, ALU.mult)
            v.tensor_tensor(lbt[:, 5, :], lbt[:, 3, :], lbt[:, 4, :], ALU.add)
            dve.drain()
            v.reciprocal(lbt[:, 5, :], lbt[:, 5, :])
            for l in range(DEPTH):
                v.scalar_tensor_tensor(vecs[:, l, V_A].rearrange("p h k -> p (h k)"), spt[:, 3, l * KD:(l + 1) * KD],
                                       4.0, spt[:, 4, l * KD:(l + 1) * KD], ALU.mult, ALU.add)
            dve.drain()
            v.tensor_tensor(lbt[:, 0, :], lbt[:, 3, :], lbt[:, 5, :], ALU.mult)
            dve.drain()
            v.tensor_scalar(lbt[:, 1, :], lbt[:, 0, :], -0.5, 0.5, ALU.mult, ALU.add)
            v.tensor_scalar(lbt[:, 2, :], lbt[:, 0, :], 0.5, 0.5, ALU.mult, ALU.add)
            dve.wait_ge(setup_act, 3)
            v.scalar_tensor_tensor(csil[:, :], csil[:, :], 1.0, cvec[:, 0, :], ALU.add, ALU.mult)
            dve.drain()
            v.tensor_scalar(csil[:, :], csil[:, :], 0.5, None, ALU.mult)
            dve.drain()
            dve.wait_ge(bada_in, 16)
            with dve.Fori(0, DEPTH) as l:
                lay = l * ROUNDS_LAYER
                ffn(lay, l * 2)
                norm(l * 3, unit_no(*at(lay, UNITS_FFN)))
                split_xT(l * 3 + 1)
                for o in (UNITS_FFN - 2, UNITS_FFN - 1):
                    turn(lay, o)
                with dve.Fori(0, 2) as hf:
                    base = lay + OFF_MIX // RING + hf * (UNITS_HALF // RING)
                    g = l * 2 + hf
                    last_bank = (len(PROJ_UNITS) - 1) % 4
                    dve.wait_ge(bank_free[last_bank], g * BANK_USES[last_bank] + 1)
                    v.memset(zpad[:, :, 0:2], 0.0)
                    v.memset(xrp[:, :, 0:3], 0.0)
                    v.tensor_copy(now[:, :, :], vecs[:, bass.ds(l, 1), :, bass.ds(hf, 1), :].rearrange(
                        "p o v h k -> p (o v h) k")).then_inc(half_start, 1)
                    for u, (name, a) in enumerate(HALF):
                        turn(base, u)
                        if name == "gates":
                            dve.wait_ge(t_done, g + 1)
                            v.tensor_scalar(rr[:, :, :], tt_[:, :, :], 1.0, None, ALU.add).then_inc(t_read, 1)
                            dve.drain()
                            v.reciprocal(rr[:, 0:2, :], rr[:, 0:2, :])
                            continue
                        hd = g * 2 + a
                        kt = bass.ds(hf * 4 + 2 * a, 2)
                        two = slice(2 * a, 2 * a + 2)
                        src, free = proj(name, a)
                        if name == "x_r":
                            dve.wait_ge(xc_part, hd + 1)
                            for tap in range(1, 4):
                                for jt in range(2):
                                    c = 2 * a + jt
                                    ins = v.scalar_tensor_tensor(xc[:, c, :], xrp[:, jt, tap:tap + T],
                                                                 now[:, V_RC + tap, c:c + 1], xc[:, c, :], ALU.mult,
                                                                 ALU.add)
                                if tap < 3:
                                    dve.drain()
                            ins.then_inc(xc_done, 1)
                            dve.wait_ge(xchi_done, hd + 1)
                            v.tensor_tensor(xclo[:, two, :], xc[:, two, :], xchi[:, two, :].bitcast(F32),
                                            ALU.subtract).then_inc(xclo_done, 1)
                        elif name == "v":
                            _, c_free = proj("c_gate", a)
                            dve.wait_ge(c_free, g * BANK_USES[proj_bank("c_gate", a)] + (
                                PROJ_UNITS.index(("c_gate", a)) // 4 + 2))
                            v.tensor_tensor(zpad[:, :, 2:], zpad[:, :, 2:], src, ALU.mult).then_inc(free, 1)
                            dve.drain()
                            for tap in range(3):
                                for jt in range(2):
                                    c = 2 * a + jt
                                    w = now[:, V_SC + tap, c:c + 1]
                                    if tap == 0:
                                        v.tensor_scalar(cv[:, jt, :], zpad[:, jt, 0:T], w, None, ALU.mult)
                                    else:
                                        ins = v.scalar_tensor_tensor(cv[:, jt, :], zpad[:, jt, tap:tap + T], w,
                                                                     cv[:, jt, :], ALU.mult, ALU.add)
                                if tap < 2:
                                    dve.drain()
                            ins.then_inc(cv_part, 1)
                        elif name == "b_gate":
                            dve.drain()
                            v.tensor_tensor(cv[:, :, :], cv[:, :, :], src, ALU.mult).then_inc(free, 1)
                            dve.drain()
                            v.memset(tick[:, :], 0.0).then_inc(cv_done, 1)
                            dve.wait_ge(yahi_done, hd + 1)
                            v.tensor_tensor(yalo[:, kt, :], cv[:, :, :], yahi[:, kt, :].bitcast(F32),
                                            ALU.subtract).then_inc(yalo_done, 1)
                        if (name, a) == ("c_gate", 0):
                            v.reciprocal(rr[:, 2:4, :], rr[:, 2:4, :])
                            dve.wait_ge(gates_read, g + 2)
                            v.scalar_tensor_tensor(gin[:, :, :], gin[:, :, :], 1.0, xc[:, :, :], ALU.add, ALU.mult)
                            dve.drain()
                        elif (name, a) == ("b_gate", 0):
                            dve.wait_ge(sqrt_done, g + 1)
                            v.tensor_tensor(tt_[:, :, :], tt_[:, :, :], rr[:, :, :], ALU.mult)
                            dve.drain()
                            v.memset(tt_[:, :, 0:1], 0.5)
                            dve.drain()
                        elif (name, a) == ("g_a", 0):
                            v.tensor_scalar(rr[:, :, :], rr[:, :, :], 2.0, -1.0, ALU.mult, ALU.add)
                            v.tensor_tensor(gin[:, :, :], gin[:, :, :], tt_[:, :, :], ALU.mult)
                            dve.drain()
                        elif (name, a) == ("g_b", 0):
                            for c in range(4):
                                v.tensor_tensor_scan(tt_[:, c, :], rr[:, c, :], gin[:, c, :], 0.0, ALU.mult, ALU.add)
                            dve.drain()
                            v.tensor_tensor(gel[:, :, :], gel[:, :, :], tt_[:, :, :], ALU.mult).then_inc(yb_done, 1)
                        elif (name, a) == ("v", 1):
                            dve.wait_ge(ybhi_done, g + 1)
                            v.tensor_tensor(yblo[:, bass.ds(hf * 4, 4), :], gel[:, :, :],
                                            ybhi[:, bass.ds(hf * 4, 4), :].bitcast(F32),
                                            ALU.subtract).then_inc(yblo_done, 1)
                base = lay + OFF_MERGE // RING
                for i, (kind, q) in enumerate(MERGE):
                    if i < UNITS_MERGE - 2:
                        turn(base, i)
                    two = slice(2 * q, 2 * q + 2)
                    if kind == "conv":
                        v.scalar_tensor_tensor(ga[:, two, :], ga[:, two, :], 1.0, halves(q), ALU.add,
                                               ALU.mult).then_inc(merged, 1)
                    elif kind == "rnn":
                        v.scalar_tensor_tensor(gb[:, two, :], gb[:, two, :], 1.0, halves(q), ALU.add,
                                               ALU.mult).then_inc(merged, 1)
                        dve.drain()
                        v.tensor_tensor(ga[:, two, :], ga[:, two, :], gb[:, two, :], ALU.add).then_inc(m_done, 1)
                        dve.wait_ge(mhi_done, l * 4 + q + 1)
                        v.scalar_tensor_tensor(xTlo[:, two, :], ga[:, two, :], 0.5, xThi[:, two, :].bitcast(F32),
                                               ALU.mult, ALU.subtract).then_inc(mlo_done, 1)
                norm(l * 3 + 1, unit_no(*at(base, UNITS_MERGE)))
                split_xT(l * 3 + 2)
                for o in (UNITS_MERGE - 2, UNITS_MERGE - 1):
                    turn(base, o)
                v.tensor_copy(csil_now[:, :], csil[:, bass.ds(l * 4, 4)])
                ffn(lay + OFF_FFN2 // RING, l * 2 + 1, l)
                norm(l * 3 + 2, unit_no(*at(lay, UNITS_LAYER)))
                split_xT(l * 3 + 3)
                for o in (UNITS_FFN - 2, UNITS_FFN - 1):
                    turn(lay + OFF_FFN2 // RING, o)
            dve_block2(dve, pieces, turn, split_xT, hid_lo, refine)


_INS = ["x", "w_in", "b_merge", "sc_w", "rc_w", "rc_b", "rg_w", "rg_b", "a_param", "w_out_conv", "w_out_rnn", "w_o",
        "ffn_w1", "ffn_w2", "ln_g", "ln_b", "c_2", "w_ada_2", "b_ada_2", "norm1_g_2", "norm2_g_2", "w_in_2",
        "lb_logits_2", "rec_out_g_2", "q_norm_g_2", "k_norm_g_2", "idx_k_norm_g_2", "idx_k_norm_b_2",
        "attn_out_g_2", "rel_bias_2", "w_out_2", "w_rg_2", "b_rg_2", "w_re_2", "b_re_2", "w1_2", "w3_2", "w2_2"]

STREAMED = ["w_in", "rg_w", "w_out_conv", "w_out_rnn", "w_o", "ffn_w1", "ffn_w2", "w_ada_2", "w_out_2", "w1_2", "w3_2",
            "w2_2"]


def kernel(**inputs):
    import concourse.bacc as _bacc
    from concourse.bass_utils import run_bass_kernel_spmd as _run

    nc = _bacc.Bacc("TRN2", target_bir_lowering=False, num_devices=1)
    arrays = {name: np.ascontiguousarray(inputs[name]) for name in _INS}
    arrays["stream"], arrays["ada"] = weight_stream(arrays)
    for name in STREAMED:
        del arrays[name]
    arrays.update(constants())
    t = {name: nc.dram_tensor(name, a.shape, mybir.dt.from_np(a.dtype), kind="ExternalInput").ap()
         for name, a in arrays.items()}
    t["scratch"] = nc.dram_tensor("scratch", [A_HEADS, HANK], F32).ap()
    out = nc.dram_tensor("out", [1, T, D], F32, kind="ExternalOutput").ap()
    build(nc, t, out)
    r = _run(nc, [arrays], core_ids=[0])
    return r.results[0]["out"]
```
